# Optimizing a Trainium2 kernel written in Bass

```python
import jax, jax.numpy as jnp
from jax import lax
import numpy as np

D_MODEL = 1024
BATCH = 1
SEQ = 512
DEPTH = 2
DEC_BATCH = 1
DEC_SEQ = 32
PAST_LEN = 512

CHUNK = 64
Q_BLOCK = 128
D_FF = 2816
N_SUB = 3
MLA_HEADS = 8
MLA_NOPE = 64
MLA_ROPE = 32
MLA_V = 64
Q_RANK = 256
KV_RANK = 128
MLA_IN = Q_RANK + KV_RANK + MLA_ROPE
RET_HEADS = 8
RET_DK = 64
RET_DV = 64
RET_IN = 2 * RET_HEADS * RET_DK + 2 * RET_HEADS * RET_DV
D_IN = MLA_IN + RET_IN
D_MIX = MLA_HEADS * MLA_V + RET_HEADS * RET_DV
ROPE_BASE = 10000.0
EPS = 1e-6
MLA_SCALE = (MLA_NOPE + MLA_ROPE) ** -0.5
RET_SCALE = RET_DK ** -0.5
NEG_INF = -1e30

kernel_name = "hybrid_mla_retention_streaming_step"

def rms_norm(x, g=None):
    xf = x.astype(jnp.float32)
    y = xf * lax.rsqrt(jnp.mean(jnp.square(xf), axis=-1, keepdims=True) + EPS)
    if g is not None:
        y = y * g.astype(jnp.float32)
    return y.astype(x.dtype)

def rope(x, pos):
    half = x.shape[-1] // 2
    inv = ROPE_BASE ** (-jnp.arange(half, dtype=jnp.float32) / half)
    ang = pos.astype(jnp.float32)[:, None] * inv[None, :]
    cos = jnp.cos(ang)[:, None, :]
    sin = jnp.sin(ang)[:, None, :]
    xf = x.astype(jnp.float32)
    x1, x2 = xf[..., :half], xf[..., half:]
    return jnp.concatenate([x1 * cos - x2 * sin, x2 * cos + x1 * sin], axis=-1).astype(x.dtype)

def swiglu(h, w1, w3, w2):
    return (jax.nn.silu(h @ w1) * (h @ w3)) @ w2

def modulated_pre(x, g, mods, j):
    return rms_norm(x, g) * (1.0 + mods[:, 3 * j + 1, None]) + mods[:, 3 * j, None]

def gated_post(x, o, g, mods, j, coef):
    return x + coef * mods[:, 3 * j + 2, None] * rms_norm(o, g)

def mla_project(z, pos, q_norm_g, kv_norm_g, w_uq, w_uk):
    b, s, _ = z.shape
    q_lat = rms_norm(z[..., :Q_RANK], q_norm_g)
    kv_lat = rms_norm(z[..., Q_RANK:Q_RANK + KV_RANK], kv_norm_g)
    k_pe = rope(z[..., Q_RANK + KV_RANK:MLA_IN][:, :, None, :], pos)[:, :, 0, :]
    q = (q_lat @ w_uq).reshape(b, s, MLA_HEADS, MLA_NOPE + MLA_ROPE)
    q_pe = rope(q[..., MLA_NOPE:], pos)
    q_abs = jnp.einsum('bshn,rhn->bshr', q[..., :MLA_NOPE],
                       w_uk.reshape(KV_RANK, MLA_HEADS, MLA_NOPE))
    return q_abs, q_pe, kv_lat, k_pe

def mla_attend(q_abs, q_pe, kv_lat, k_pe, q_pos, k_pos):
    s = jnp.einsum('bqhr,bkr->bhqk', q_abs, kv_lat) + jnp.einsum('bqhd,bkd->bhqk', q_pe, k_pe)
    s = s.astype(jnp.float32) * MLA_SCALE
    allowed = (k_pos[None, :] // CHUNK) <= (q_pos[:, None] // CHUNK)
    p = jax.nn.softmax(jnp.where(allowed, s, NEG_INF), axis=-1).astype(kv_lat.dtype)
    return jnp.einsum('bhqk,bkr->bqhr', p, kv_lat)

def mla_output(o_lat, w_uv):
    b, s = o_lat.shape[:2]
    o = jnp.einsum('bshr,rhv->bshv', o_lat, w_uv.reshape(KV_RANK, MLA_HEADS, MLA_V))
    return o.reshape(b, s, MLA_HEADS * MLA_V)

def ret_project(z, pos):
    b, s, _ = z.shape
    hk, hv = RET_HEADS * RET_DK, RET_HEADS * RET_DV
    q = rope(z[..., :hk].reshape(b, s, RET_HEADS, RET_DK), pos)
    k = rope(z[..., hk:2 * hk].reshape(b, s, RET_HEADS, RET_DK), pos) * RET_SCALE
    v = z[..., 2 * hk:2 * hk + hv].reshape(b, s, RET_HEADS, RET_DV)
    g = z[..., 2 * hk + hv:]
    return q, k, v, g

def retention_block(state, q, k, v):
    t = q.shape[1]
    log_g = jnp.log1p(-jnp.exp2(-5.0 - jnp.arange(RET_HEADS, dtype=jnp.float32)))
    n = jnp.arange(t, dtype=jnp.float32)
    diff = n[:, None] - n[None, :]
    decay = jnp.where(diff >= 0.0, jnp.exp(jnp.maximum(diff, 0.0)[None] * log_g[:, None, None]), 0.0)
    qf, kf, vf = q.astype(jnp.float32), k.astype(jnp.float32), v.astype(jnp.float32)
    scores = jnp.einsum('bnhd,bmhd->bhnm', qf, kf) * decay[None]
    o = jnp.einsum('bhnm,bmhv->bnhv', scores, vf)
    cross = jnp.exp((n + 1.0)[:, None] * log_g[None, :])
    o = o + jnp.einsum('bnhd,bhdv->bnhv', qf, state) * cross[None, :, :, None]
    k_dec = kf * jnp.exp((t - 1.0 - n)[:, None] * log_g[None, :])[None, :, :, None]
    new_state = jnp.exp(t * log_g)[None, :, None, None] * state + jnp.einsum('bmhd,bmhv->bhdv', k_dec, vf)
    return new_state, o

def ret_output(o, g):
    b, s = o.shape[:2]
    return rms_norm(o).reshape(b, s, RET_HEADS * RET_DV).astype(g.dtype) * jax.nn.silu(g)

def setup_inputs(seed: int = 0) -> dict:
    key = jax.random.key(seed)
    ks = jax.random.split(key, 24)
    f32 = jnp.float32
    nrm = lambda k, shape, scale: jax.random.normal(k, shape, f32) * scale
    return {
        'x_prompt': nrm(ks[0], (BATCH, SEQ, D_MODEL), 1.0),
        'x_sample': nrm(ks[1], (DEC_BATCH, DEC_SEQ, D_MODEL), 1.0),
        'cache_kv_latent': nrm(ks[2], (DEPTH, DEC_BATCH, PAST_LEN, KV_RANK), 1.0),
        'cache_k_rope': nrm(ks[3], (DEPTH, DEC_BATCH, PAST_LEN, MLA_ROPE), 1.0),
        'state_ret': nrm(ks[4], (DEPTH, DEC_BATCH, RET_HEADS, RET_DK, RET_DV), 0.5),
        'c_prompt': nrm(ks[5], (BATCH, D_MODEL), 1.0),
        'c_sample': nrm(ks[6], (DEC_BATCH, D_MODEL), 1.0),
        'ada_w': nrm(ks[7], (DEPTH, D_MODEL, 3 * N_SUB * D_MODEL), 0.3 * D_MODEL ** -0.5),
        'ada_b': nrm(ks[8], (DEPTH, 3 * N_SUB * D_MODEL), 0.02),
        'norm_pre': 1.0 + nrm(ks[9], (DEPTH, N_SUB, D_MODEL), 0.05),
        'norm_post': 1.0 + nrm(ks[10], (DEPTH, N_SUB, D_MODEL), 0.05),
        'ffn_w1': nrm(ks[11], (DEPTH, 2, D_MODEL, D_FF), D_MODEL ** -0.5),
        'ffn_w3': nrm(ks[12], (DEPTH, 2, D_MODEL, D_FF), D_MODEL ** -0.5),
        'ffn_w2': nrm(ks[13], (DEPTH, 2, D_FF, D_MODEL), D_FF ** -0.5),
        'w_in': nrm(ks[14], (DEPTH, D_MODEL, D_IN), D_MODEL ** -0.5),
        'q_norm': 1.0 + nrm(ks[15], (DEPTH, Q_RANK), 0.05),
        'kv_norm': 1.0 + nrm(ks[16], (DEPTH, KV_RANK), 0.05),
        'w_uq': nrm(ks[17], (DEPTH, Q_RANK, MLA_HEADS * (MLA_NOPE + MLA_ROPE)), Q_RANK ** -0.5),
        'w_uk': nrm(ks[18], (DEPTH, KV_RANK, MLA_HEADS * MLA_NOPE), KV_RANK ** -0.5),
        'w_uv': nrm(ks[19], (DEPTH, KV_RANK, MLA_HEADS * MLA_V), KV_RANK ** -0.5),
        'w_out': nrm(ks[20], (DEPTH, D_MIX, D_MODEL), D_MIX ** -0.5),
    }

def reference(x_prompt, x_sample, cache_kv_latent, cache_k_rope, state_ret, c_prompt, c_sample,
              ada_w, ada_b, norm_pre, norm_post, ffn_w1, ffn_w3, ffn_w2,
              w_in, q_norm, kv_norm, w_uq, w_uk, w_uv, w_out):

    def mixer_prompt(h, l):
        b, s, _ = h.shape
        pos = jnp.arange(s, dtype=jnp.int32)
        z = h @ w_in[l]
        q_abs, q_pe, kv_lat, k_pe = mla_project(z[..., :MLA_IN], pos, q_norm[l], kv_norm[l], w_uq[l], w_uk[l])
        nb = s // Q_BLOCK
        qa = q_abs.reshape(b, nb, Q_BLOCK, MLA_HEADS, KV_RANK).swapaxes(0, 1)
        qp = q_pe.reshape(b, nb, Q_BLOCK, MLA_HEADS, MLA_ROPE).swapaxes(0, 1)
        qpos = pos.reshape(nb, Q_BLOCK)
        o_lat = lax.map(lambda a: mla_attend(a[0], a[1], kv_lat, k_pe, a[2], pos), (qa, qp, qpos))
        o_lat = o_lat.swapaxes(0, 1).reshape(b, s, MLA_HEADS, KV_RANK)
        o_mla = mla_output(o_lat, w_uv[l])
        q, k, v, g = ret_project(z[..., MLA_IN:], pos)
        nc = s // CHUNK
        to_blocks = lambda t: t.reshape(b, nc, CHUNK, *t.shape[2:]).swapaxes(0, 1)
        r0 = jnp.zeros((b, RET_HEADS, RET_DK, RET_DV), jnp.float32)
        r_fin, o_ret = lax.scan(lambda r, xs: retention_block(r, xs[0], xs[1], xs[2]), r0,
                                (to_blocks(q), to_blocks(k), to_blocks(v)))
        o_ret = ret_output(o_ret.swapaxes(0, 1).reshape(b, s, RET_HEADS, RET_DV), g)
        out = jnp.concatenate([o_mla, o_ret], axis=-1) @ w_out[l]
        return out, (kv_lat, k_pe, r_fin.astype(h.dtype))

    def mixer_sample(h, l):
        t = h.shape[1]
        pos = PAST_LEN + jnp.arange(t, dtype=jnp.int32)
        z = h @ w_in[l]
        q_abs, q_pe, kv_lat, k_pe = mla_project(z[..., :MLA_IN], pos, q_norm[l], kv_norm[l], w_uq[l], w_uk[l])
        kv_all = jnp.concatenate([cache_kv_latent[l].astype(kv_lat.dtype), kv_lat], axis=1)
        kpe_all = jnp.concatenate([cache_k_rope[l].astype(k_pe.dtype), k_pe], axis=1)
        k_pos = jnp.arange(PAST_LEN + t, dtype=jnp.int32)
        o_mla = mla_output(mla_attend(q_abs, q_pe, kv_all, kpe_all, pos, k_pos), w_uv[l])
        q, k, v, g = ret_project(z[..., MLA_IN:], pos)
        r_new, o_ret = retention_block(state_ret[l].astype(jnp.float32), q, k, v)
        o_ret = ret_output(o_ret, g)
        out = jnp.concatenate([o_mla, o_ret], axis=-1) @ w_out[l]
        return out, (kv_lat, k_pe, r_new.astype(h.dtype))

    def layer(x, c, l, mixer):
        mods = (jax.nn.silu(c) @ ada_w[l] + ada_b[l]).reshape(c.shape[0], 3 * N_SUB, D_MODEL)
        h = modulated_pre(x, norm_pre[l, 0], mods, 0)
        x = gated_post(x, swiglu(h, ffn_w1[l, 0], ffn_w3[l, 0], ffn_w2[l, 0]), norm_post[l, 0], mods, 0, 0.5)
        h = modulated_pre(x, norm_pre[l, 1], mods, 1)
        o, st = mixer(h, l)
        x = gated_post(x, o, norm_post[l, 1], mods, 1, 1.0)
        h = modulated_pre(x, norm_pre[l, 2], mods, 2)
        x = gated_post(x, swiglu(h, ffn_w1[l, 1], ffn_w3[l, 1], ffn_w2[l, 1]), norm_post[l, 2], mods, 2, 0.5)
        return x, st

    y_prompt, y_sample = x_prompt, x_sample
    lat_p, kpe_p, ret_p, lat_s, kpe_s, ret_s = [], [], [], [], [], []
    for l in range(DEPTH):
        y_prompt, (a, b_, r) = layer(y_prompt, c_prompt, l, mixer_prompt)
        lat_p.append(a); kpe_p.append(b_); ret_p.append(r)
        y_sample, (a, b_, r) = layer(y_sample, c_sample, l, mixer_sample)
        lat_s.append(a); kpe_s.append(b_); ret_s.append(r)
    new_kv_latent_prompt = jnp.stack(lat_p)
    new_k_rope_prompt = jnp.stack(kpe_p)
    new_state_ret_prompt = jnp.stack(ret_p)
    new_kv_latent_sample = jnp.stack(lat_s)
    new_k_rope_sample = jnp.stack(kpe_s)
    new_state_ret_sample = jnp.stack(ret_s)
    return (y_prompt, y_sample, new_kv_latent_prompt, new_k_rope_prompt, new_state_ret_prompt,
            new_kv_latent_sample, new_k_rope_sample, new_state_ret_sample)


_drawn_inputs = setup_inputs


def setup_inputs(seed=0):
    import zlib

    import numpy as np

    out = dict(_drawn_inputs(seed))
    spreads = {}
    factors = {'cache_k_rope': 3.931, 'norm_post': 3.379, 'q_norm': 8.0}
    for name, (base, spread) in spreads.items():
        noise = np.random.default_rng([zlib.crc32(name.encode()), seed]).standard_normal(out[name].shape)
        drawn = base * np.exp(spread * noise) if base else spread * noise
        out[name] = __import__('jax').numpy.asarray(drawn.astype(out[name].dtype))
    for name, factor in factors.items():
        out[name] = (out[name] * factor).astype(out[name].dtype)
    return out
```

```python
from contextlib import ExitStack

import numpy as np

import concourse.bass as bass
from concourse import mybir

F32 = mybir.dt.float32
F32R = mybir.dt.float32r
BF16 = mybir.dt.bfloat16
ALU = mybir.AluOpType
ACT = mybir.ActivationFunctionType
AX = mybir.AxisListType

P = 128
D = 1024
DEPTH = 2
NP_, NS = 512, 32
T = NP_ + NS
HT = T // 2
PAST = 512
D_FF = 2816
KD = D // P
FT = D_FF // P
HEADS = 8
NOPE, ROPE, VD = 64, 32, 64
Q_RANK, KV_RANK = 256, 128
RDK = 64
EPS = 1e-6
MLA_SCALE = float((NOPE + ROPE) ** -0.5)
RET_SCALE = float(RDK ** -0.5)
NEG = -1e30

DN_T = FT // 2
UP_C = 2 * FT
DN_C = 2 * KD
Z_EARLY = 5
Z_C = Z_EARLY + 16
UQ_C = 2
MIX_C = Z_C + UQ_C + 1 + KD
OUT_C0 = Z_C + UQ_C + 1
CH = UP_C + DN_C + MIX_C + UP_C + DN_C
FFN_C = (0, UP_C + DN_C + MIX_C)
MIX_C0 = UP_C + DN_C
assert CH % 2 == 0 and UP_C % 4 == 0 and DN_C % 4 == 0 and MIX_C % 4 == 0

MODS = 9 * KD
ADA_RING = 4
ADA_A = 48
ADA_B = 24


COL_A = 2 * ADA_A // ADA_RING + 8
COL_B = 2 * ADA_B // ADA_RING + 4
N_CONST = 11


class Signal:

    def __init__(self, sem, per_layer, before=0):
        self.sem, self.per_layer, self.before = sem, per_layer, before

    def at(self, layer, n):
        return layer * self.per_layer + (self.before + n)


def streaming_trunk(nc, a, o):
    ctx = ExitStack()
    with ctx:
        def sb(name, shape, dt=F32):
            return ctx.enter_context(nc.sbuf_tensor(name, shape, dt))

        def overlay(alternatives):
            made, size = {}, 0
            for group in alternatives:
                with ExitStack() as scope:
                    total = 0
                    for item in group:
                        if isinstance(item, list):
                            inner, more = overlay(item)
                            made.update(inner)
                            total += more
                        else:
                            name, shape, dt = item
                            made[name] = scope.enter_context(nc.sbuf_tensor(name, shape, dt))
                            total += int(np.prod(shape[1:])) * 4
                    size = max(size, total)
            return made, size

        def signal(name, per_layer, before=0):
            return Signal(ctx.enter_context(nc.semaphore(name)), per_layer, before)

        x = sb("x", [P, KD, T])
        c_all = sb("c_all", [P, 2, D])
        raw = sb("raw", [P, 2, DN_T * P])
        w_hi = sb("w_hi", [P, 2, DN_T * P], F32R)
        w_lo = sb("w_lo", [P, 2, DN_T * P], F32R)
        tmp_s = sb("tmp_s", [P, 2, T])
        tmp_v = sb("tmp_v", [P, 2, T])
        root = sb("root", [P, T])
        rinv = sb("rinv", [P, T])
        ones = sb("ones", [P, P])
        mods = sb("mods", [P, 2, MODS])
        mul_pre = sb("mul_pre", [P, 3, 2, KD])
        mul_post = sb("mul_post", [P, 3, 2, KD])
        row_max, neg_max, exp_sum, inv_sum = (sb(n, [P, 4]) for n in ("row_max", "neg_max", "exp_sum", "inv_sum"))
        acc = sb("acc", [P, 2, ADA_RING])
        gains = sb("gains", [P, 3])
        junk = [tmp_v[:, v, :].bitcast(BF16)[:, 0:D] for v in range(2)]

        ident = sb("ident", [P, P])
        half_ones = sb("half_ones", [P, P])
        k_decay = sb("k_decay", [P, 2, 4, 4])
        k_decays = sb("k_decays", [NS, HEADS])
        cross = sb("cross", [P, 2, 4, NS])
        own_head = sb("own_head", [P, 4, NS])
        state_decay = sb("state_decay", [P, 2])
        ada_b = sb("ada_b", [P, DEPTH * MODS + 16])
        g_pre = sb("g_pre", [P, DEPTH * 3 * KD + KD])
        g_post = sb("g_post", [P, DEPTH * 3 * KD])
        g_lat = sb("g_lat", [P, DEPTH * 3])
        eps = sb("eps", [P, 1])
        neg_row = sb("neg_row", [P, 64])
        scratch = sb("scratch", [P, 14])

        hm, size = overlay([
            [("h_hi", [P, KD, T], F32R), ("h_lo", [P, KD, T], F32R)],
            [("o_ffn", [P, KD, T], F32), ("ada_w", [P, ADA_RING, D], F32)],
            [("decay", [P, HEADS, 512], F32), ("q_cross", [P, 4, 4, NS], F32), ("ret_ss", [NS, HEADS, NS], F32),
             ("k_toks", [NS, 4, P], F32)],
            [("mla_hi", [P, 4, T], F32R), ("mla_lo", [P, 4, T], F32R),
             ("ret_hi", [P, 4, T], F32R), ("ret_lo", [P, 4, T], F32R)],
        ])
        sb("h_space", [P, size // 4])
        h_hi, h_lo, o_ffn, ada_w = hm["h_hi"], hm["h_lo"], hm["o_ffn"], hm["ada_w"]
        decay, mla_hi, mla_lo, ret_hi, ret_lo = hm["decay"], hm["mla_hi"], hm["mla_lo"], hm["ret_hi"], hm["ret_lo"]

        um, size = overlay([
            [("u_hi", [P, FT, T], F32R), ("u_lo", [P, FT, T], F32R)],
            [("kv", [P, T], F32), ("kpe", [P, T], F32), ("q_nope", [P, 4, T], F32), ("q_pe", [P, 2, T], F32),
             ("ret_v", [P, 4, T], F32), ("ret_g", [P, 4, T], F32), ("kv_tok", [P, 5, P], F32),
             ("w_ukv", [P, 8, P], F32), ("state_in", [P, 4, VD], F32), ("state_p", [P, 4, VD], F32),
             [[("ret_q", [P, 4, T], F32), ("ret_k", [P, 4, T], F32), ("kpe_swap", [P, T], F32),
               ("q_pe_swap", [P, 2, T], F32), ("rope_tab", [P, 4, T], F32), ("v_tok", [P, 5, 512], F32),
               [[("zq", [P, 2, T], F32), ("qn_hi", [P, 2, T], F32R), ("qn_lo", [P, 2, T], F32R)],
                [("k_tok", [P, 4, P], F32), ("ret_st", [P, 4, 512], F32)]]],
              [("q_abs", [P, HEADS, 512], F32), ("q_abss", [P, HEADS, NS], F32), ("q_pes", [P, 2, 4, NS], F32), ("pt", [P, 2, 4, 512], F32), ("prob", [P, 4, T], F32),
               ("o_lat", [P, 2, 512], F32), ("o_lats", [P, HEADS, NS], F32), ("cache_kv", [P, T], F32),
               ("cache_pe", [P, T], F32), ("cache_tok", [P, 4, P], F32)]]],
            [("o_mix", [P, KD, T], F32)],
        ])
        sb("u_space", [P, size // 4])
        u_hi, u_lo, kv, kpe, q_nope, q_pe = (um[n] for n in ("u_hi", "u_lo", "kv", "kpe", "q_nope", "q_pe"))
        ret_v, ret_g, kv_tok, w_ukv, ret_q, ret_k = (
            um[n] for n in ("ret_v", "ret_g", "kv_tok", "w_ukv", "ret_q", "ret_k"))
        kpe_swap, q_pe_swap, rope_tab, v_tok, state_in, zq = (
            um[n] for n in ("kpe_swap", "q_pe_swap", "rope_tab", "v_tok", "state_in", "zq"))
        qn_hi, qn_lo, k_tok, state_p, ret_st = (um[n] for n in ("qn_hi", "qn_lo", "k_tok", "state_p", "ret_st"))
        q_cross, ret_ss, k_toks = hm["q_cross"], hm["ret_ss"], hm["k_toks"]
        q_abs, q_abss, q_pes, pt, prob, o_lat = (um[n] for n in ("q_abs", "q_abss", "q_pes", "pt", "prob", "o_lat"))
        o_lats, cache_kv, cache_pe, cache_tok, o_mix = (
            um[n] for n in ("o_lats", "cache_kv", "cache_pe", "cache_tok", "o_mix"))

        ps = ctx.enter_context(nc.psum_tensor("ps", [P, 8, 512], F32))

        def pair(b):
            return ps[:, b:b + 2, 0:HT]

        def halves(t):
            return t.rearrange("p (t n) -> p t n", t=2)

        landed = [signal(f"landed{i}", 16 * CH // 2) for i in range(2)]
        hi_done = signal("hi_done", CH)
        lo_done = signal("lo_done", CH, 2)
        w_used = signal("w_used", CH, 2)
        ada_landed = [signal(f"ada_landed{i}", 16 * MODS // ADA_RING, 16 * 16 // ADA_RING) for i in range(ADA_RING)]
        ada_done = signal("ada_done", 2 * MODS, 2 * 16)
        columns = signal("columns", COL_A + COL_B, 10)
        x_prod = signal("x_prod", 48)
        x_new = signal("x_new", 24, 8)
        x_sq = signal("x_sq", 24)
        sums = signal("sums", 48, 2)
        rooted = signal("rooted", 6)
        inverted = signal("inverted", 6)
        h_scaled = signal("h_scaled", 48)
        h_high = signal("h_high", 48)
        h_ready = signal("h_ready", 48)
        up_silu = signal("up_silu", 2 * FT)
        up_mul = signal("up_mul", 2 * FT, 2)
        up_hi = signal("up_hi", 2 * FT)
        up_lo = signal("up_lo", 2 * FT, 2)
        out_ev = signal("out_ev", 24)
        out_sq = signal("out_sq", 24)
        z_ev = signal("z_ev", Z_C)
        m_sq = signal("m_sq", 7)
        m_sum = signal("m_sum", 7)
        m_root = signal("m_root", 6)
        m_inv = signal("m_inv", 6)
        q_scaled = signal("q_scaled", 2)
        q_high = signal("q_high", 2)
        q_low = signal("q_low", 2)
        kv_ready = signal("kv_ready", 1)
        tables = signal("tables", 16 * 2)
        decay_in = signal("decay_in", 16)
        caches = signal("caches", 16 * 3)
        rope = signal("rope", 33)
        uq_mm = signal("uq_mm", 6)
        gains_in = signal("gains_in", 1)
        uq_ev = signal("uq_ev", 8)
        ukv_in = signal("ukv_in", 1)
        tok_mm = signal("tok_mm", 7)
        tok_ev = signal("tok_ev", 7)
        kt_mm = signal("kt_mm", 5)
        kt_ev = signal("kt_ev", 6)
        rs_mm = signal("rs_mm", 4 * HEADS)
        rs_mul = signal("rs_mul", 4 * HEADS)
        ro_mm = signal("ro_mm", HEADS)
        ro_ev = signal("ro_ev", 4)
        ss_mm = signal("ss_mm", 1)
        ss_mul = signal("ss_mul", 3)
        so_mm = signal("so_mm", 1)
        so_ev = signal("so_ev", 1)
        st_mm = signal("st_mm", 4)
        st_ev = signal("st_ev", 4 * 8)
        ret_prod = signal("ret_prod", 8)
        ret_high = signal("ret_high", 4)
        ret_low = signal("ret_low", 4)
        qa_mm = signal("qa_mm", HEADS)
        qa_ev = signal("qa_ev", HEADS)
        SU = 4 * HEADS + 2
        sc_mm = signal("sc_mm", SU)
        sc_max = signal("sc_max", 2 * SU)
        sc_exp = signal("sc_exp", SU)
        sc_norm = signal("sc_norm", 2 * SU)
        at_mm = signal("at_mm", SU)
        at_ev = signal("at_ev", SU)
        pv_mm = signal("pv_mm", HEADS + 2)
        pv_ev = signal("pv_ev", HEADS + 2)
        uv_mm = signal("uv_mm", 5)
        uv_hi = signal("uv_hi", 5)
        uv_lo = signal("uv_lo", 5)
        cache_new = signal("cache_new", 4)
        stored = signal("stored", 16 * 4)
        const_in = signal("const_in", 0)
        x_in = signal("x_in", 0)
        c_in = signal("c_in", 0)
        c_act = signal("c_act", 0)
        filled = signal("filled", 0)
        y_out = signal("y_out", 0)

        ITEMS = [("p", 0), ("p", 1), ("p", 2), ("p", 3), ("s", 0), ("p", 4), ("p", 5), ("s", 1), ("p", 6), ("p", 7)]
        FIRST_UNIT = []
        n_units = 0
        for kind, _ in ITEMS:
            FIRST_UNIT.append(n_units)
            n_units += 4 if kind == "p" else 1
        ITEM_OF = {it: i for i, it in enumerate(ITEMS)}

        block = ctx.enter_context(nc.Block())

        @block.sync
        def _(sp):
            def load_ada(tile, slot):
                sp.dma_start(ada_w[:, slot, :], a["ada"][bass.ds(tile, 1)].rearrange("a p n -> p (a n)"))\
                    .then_inc(ada_landed[slot].sem, 16)

            def load_chunk(l, c, slot, src, width):
                sp.wait_ge(lo_done.sem, lo_done.at(l, c - 1))
                sp.dma_start(raw[:, slot, 0:width], src.rearrange("a p n -> p (a n)"))\
                    .then_inc(landed[slot].sem, 16)

            sp.dma_start(c_all[:, :, :], a["c"].partition_broadcast(P)).then_inc(c_in.sem, 16)
            for t in range(ADA_RING):
                load_ada(t, t)
            sp.dma_start(x[:, :, :], a["x"]).then_inc(x_in.sem, 16)
            consts = [(ident, "ident"), (half_ones, "half_ones"), (k_decay, "k_decay"), (k_decays, "k_decays"),
                      (cross, "cross"), (own_head, "own_head"), (state_decay, "state_decay"), (ada_b, "ada_b"), (g_pre, "g_pre"),
                      (g_post, "g_post"), (g_lat, "g_lat")]
            for t, n in consts:
                sp.dma_start(t[tuple([slice(None)] * len(t.shape))], a[n]).then_inc(const_in.sem, 16)
            for t in range(ADA_RING, 16):
                sp.wait_ge(ada_done.sem, 2 * (t - ADA_RING + 1))
                load_ada(t, t % ADA_RING)

            def ffn(l, s):
                base = FFN_C[s]
                with sp.Fori(0, UP_C // 2) as i:
                    for k in range(2):
                        load_chunk(l, base + i * 2 + k, k, a["w_up"][bass.ds((l * 2 + s) * UP_C + i * 2 + k, 1)], KD * P)
                first, per = ((0, ADA_A // 4), (ADA_A, ADA_B // 3))[s]

                def down(i, first_time=False, ada=True):
                    for k in range(4):
                        load_chunk(l, base + UP_C + i * 4 + k, k % 2,
                                   a["w_dn"][bass.ds((l * 2 + s) * DN_C + i * 4 + k, 1)], DN_T * P)
                        for t in range(k * per // 4, (k + 1) * per // 4) if ada else ():
                            if not first_time or t >= ADA_RING:
                                sp.wait_ge(ada_done.sem, ada_done.at(l, 2 * first + 2 * per * i + 2 * (t - ADA_RING + 1)))
                            elif t == 0:
                                sp.wait_ge(w_used.sem, w_used.at(l, base + UP_C))
                            load_ada(l * MODS + 16 + first + i * per + t, t % ADA_RING)

                down(0, first_time=True)
                with sp.Fori(1, 4 - s) as i:
                    down(i)
                if s == 1:
                    down(3, ada=False)

            with sp.Fori(0, DEPTH) as l:
                ffn(l, 0)
                for c in range(MIX_C):
                    load_chunk(l, MIX_C0 + c, c % 2, a["w_mix"][bass.ds(l * MIX_C + c, 1)], KD * P)
                    if c == 1:
                        sp.wait_ge(w_used.sem, w_used.at(l, MIX_C0))
                        sp.dma_start(rope_tab[:, :, :], a["rope"]).then_inc(tables.sem, 16)
                        sp.dma_start(state_in[:, :, :], a["state"][bass.ds(l, 1)].rearrange("a p i v -> p (a i) v"))\
                            .then_inc(tables.sem, 16)
                    if c == Z_C + 1:
                        sp.wait_ge(w_used.sem, w_used.at(l, MIX_C0 + Z_C))
                        sp.dma_start(decay[:, :, :], a["decay"]).then_inc(decay_in.sem, 16)
                    if c == OUT_C0 + 1:
                        sp.wait_ge(kv_ready.sem, kv_ready.at(l, 1))
                        sp.dma_start(o["kv"][bass.ds(l, 1)].rearrange("a p n -> p (a n)"), kv[:, :]).then_inc(stored.sem, 16)
                        sp.wait_ge(rope.sem, rope.at(l, 3))
                        sp.dma_start(o["kpe"][bass.ds(l, 1)].rearrange("a p n -> p (a n)"), kpe[0:ROPE, :]).then_inc(stored.sem, 16)
                        sp.wait_ge(st_ev.sem, st_ev.at(l, 32))
                        sp.dma_start(o["state_p"][bass.ds(l, 1)].rearrange("a p i v -> p (a i) v"), state_p[:, :, :])\
                            .then_inc(stored.sem, 16)
                        sp.dma_start(o["state_s"][bass.ds(l, 1)].rearrange("a p i v -> p (a i) v"), state_in[:, :, :])\
                            .then_inc(stored.sem, 16)
                        sp.wait_ge(ro_mm.sem, ro_mm.at(l, HEADS))
                        sp.dma_start(cache_kv[:, 0:PAST], a["cache_kv"][bass.ds(l, 1)].rearrange("a p n -> p (a n)"))\
                            .then_inc(caches.sem, 16)
                        sp.dma_start(cache_pe[:, 0:PAST], a["cache_pe"][bass.ds(l, 1)].rearrange("a p n -> p (a n)"))\
                            .then_inc(caches.sem, 16)
                        sp.dma_start(cache_tok[:, :, :], a["cache_tok"][bass.ds(l, 1)].rearrange("a p b r -> p (a b) r"))\
                            .then_inc(caches.sem, 16)
                ffn(l, 1)
            sp.wait_ge(x_new.sem, x_new.at(DEPTH, 0))
            sp.dma_start(o["y"], x[:, :, :]).then_inc(y_out.sem, 16)
            sp.wait_ge(y_out.sem, 16)
            sp.wait_ge(stored.sem, stored.at(DEPTH, 0))

        @block.gpsimd
        def _(pool):
            for k in range(2):
                pool.memset(scratch[:, k:k + 1], 0.0).then_inc(lo_done.sem, 1)

            def low(l, c, slot, width):
                pool.wait_ge(hi_done.sem, hi_done.at(l, c + 1))
                pool.tensor_tensor(w_lo[:, slot, 0:width], raw[:, slot, 0:width], w_hi[:, slot, 0:width].bitcast(F32),
                                   ALU.subtract).then_inc(lo_done.sem, 1)

            def ffn(l, s):
                with pool.Fori(0, UP_C // 2) as i:
                    for k in range(2):
                        low(l, FFN_C[s] + i * 2 + k, k, KD * P)
                with pool.Fori(0, DN_C // 2) as i:
                    for k in range(2):
                        low(l, FFN_C[s] + UP_C + i * 2 + k, k, DN_T * P)

            with pool.Fori(0, DEPTH) as l:
                ffn(l, 0)
                with pool.Fori(0, MIX_C // 2) as i:
                    for k in range(2):
                        low(l, MIX_C0 + i * 2 + k, k, KD * P)
                ffn(l, 1)

        @block.tensor
        def _(pe):
            pe.wait_ge(filled.sem, 1)
            for n, sig in enumerate((w_used, sums)):
                for k in range(2):
                    pe.matmul(ps[:, 2 * n + k, 0:P], ones[:, :], ones[:, :], start=True, stop=True).then_inc(sig.sem, 1)

            def tile3(bank, slot, kk, hi, lo, start, stop):
                wh = w_hi[:, slot, kk * P:(kk + 1) * P]
                wl = w_lo[:, slot, kk * P:(kk + 1) * P]
                for t in range(2):
                    n = slice(t * HT, (t + 1) * HT)
                    pe.matmul(ps[:, bank + t, 0:HT], wh, hi[:, n], start=start, stop=False)
                    pe.matmul(ps[:, bank + t, 0:HT], wh, lo[:, n], start=False, stop=False)
                for t in range(2):
                    n = slice(t * HT, (t + 1) * HT)
                    last = pe.matmul(ps[:, bank + t, 0:HT], wl, hi[:, n], start=False, stop=stop)
                return last

            def add_squares(src, bank, start, stop, mat):
                for t in range(2):
                    last = pe.matmul(ps[:, bank + t, 0:HT], mat[:, :], src[:, t * HT:(t + 1) * HT],
                                     start=start, stop=stop)
                return last

            def pre_norm(l, j):
                for m in range(KD):
                    pe.wait_ge(x_sq.sem, x_sq.at(l, j * KD + m + 1))
                    add_squares(tmp_s[:, m % 2, :], 6, m == 0, m == KD - 1, ones).then_inc(sums.sem, 1)

            def up(l, s):
                base = FFN_C[s]
                with pe.Fori(0, FT // 2) as i:
                    for f in range(2):
                        pe.wait_ge(up_mul.sem, up_mul.at(l, s * FT + i * 2 + f - 1))
                        for w in range(2):
                            pe.wait_ge(lo_done.sem, lo_done.at(l, base + i * 4 + 2 * f + w + 1))
                            for k in range(KD):
                                if f == 0 and w == 0:
                                    pe.wait_ge(h_ready.sem, h_ready.at(l, (2 * s) * 16 + 2 * k + 2))
                                last = tile3(4 * f + 2 * w, w, k, h_hi[:, k, :], h_lo[:, k, :], k == 0, k == KD - 1)
                            last.then_inc(w_used.sem, 1)

            def out_tiles(l, j, chunk0, per_tile, chunk_tiles, operand, ready):
                def squares(m, mm, start, stop):
                    pe.wait_ge(out_sq.sem, out_sq.at(l, j * KD + m + 1))
                    add_squares(tmp_s[:, mm, :], 4, start, stop, ones).then_inc(sums.sem, 1)

                def tile(m, mm, first):
                    if not first:
                        pe.wait_ge(out_sq.sem, out_sq.at(l, j * KD + m - 1))
                    k = 0
                    for q in range(per_tile):
                        n = m * per_tile + q
                        pe.wait_ge(lo_done.sem, lo_done.at(l, chunk0 + n + 1))
                        for kk in range(chunk_tiles):
                            if first:
                                ready(k)
                            hi, lo = operand(k)
                            last = tile3(2 * mm, (q + mm * per_tile + chunk0) % 2, kk, hi, lo,
                                         k == 0, k == per_tile * chunk_tiles - 1)
                            k += 1
                        last.then_inc(w_used.sem, 1)

                tile(0, 0, True)
                tile(1, 1, True)
                squares(0, 0, True, False)
                with pe.Fori(1, KD // 2) as i:
                    tile(i * 2, 0, False)
                    squares(i * 2 - 1, 1, False, False)
                    tile(i * 2 + 1, 1, False)
                    squares(i * 2, 0, False, False)
                squares(KD - 1, 1, False, True)

            def ffn(l, s):
                pre_norm(l, 2 * s)
                up(l, s)

                def ready(k):
                    if k in (0, FT - 2, FT - 1):
                        pe.wait_ge(up_lo.sem, up_lo.at(l, s * FT + max(k + 1, FT - 2)))

                out_tiles(l, 2 * s, FFN_C[s] + UP_C, 2, DN_T, lambda k: (u_hi[:, k, :], u_lo[:, k, :]), ready)

            def mixer(l):
                pre_norm(l, 1)

                def z_tile(z, bank, slot, first):
                    if not first:
                        pe.wait_ge(z_ev.sem, z_ev.at(l, z - 1))
                    pe.wait_ge(lo_done.sem, lo_done.at(l, MIX_C0 + z + 1))
                    for k in range(KD):
                        if first:
                            pe.wait_ge(h_ready.sem, h_ready.at(l, 16 + 2 * k + 2))
                        last = tile3(bank, slot, k, h_hi[:, k, :], h_lo[:, k, :], k == 0, k == KD - 1)
                    last.then_inc(w_used.sem, 1)

                def norm_sum(n, buf, bank, start, stop, mat=ones):
                    pe.wait_ge(m_sq.sem, m_sq.at(l, n + 1))
                    add_squares(tmp_s[:, buf, :], bank, start, stop, mat).then_inc(m_sum.sem, 1)

                for z in range(Z_EARLY):
                    z_tile(z, 2 * (z % 2), z % 2, z < 2)
                    if z == 2:
                        norm_sum(0, 0, 4, True, False)
                        norm_sum(1, 1, 4, False, True)
                    if z == 3:
                        norm_sum(2, 0, 6, True, True)
                with pe.Fori(0, 4) as i:
                    for t in range(4):
                        z = Z_EARLY + t
                        z_tile(i * 4 + z, 2 * (z % 2), z % 2, False)

                for c in range(UQ_C):
                    pe.wait_ge(lo_done.sem, lo_done.at(l, MIX_C0 + Z_C + c + 1))
                    for oo in range(4):
                        n = 4 * c + oo
                        if n < 2:
                            pe.wait_ge(z_ev.sem, z_ev.at(l, Z_C))
                        else:
                            pe.wait_ge(uq_ev.sem, uq_ev.at(l, n - 1))
                        for k in range(2):
                            if n == 0:
                                pe.wait_ge(q_low.sem, q_low.at(l, k + 1))
                            last = tile3(2 * (n % 2), (Z_C + c) % 2, 2 * oo + k, qn_hi[:, k, :], qn_lo[:, k, :],
                                         k == 0, k == 1)
                        last.then_inc((w_used if oo == 3 else uq_mm).sem, 1)

                pe.wait_ge(ukv_in.sem, ukv_in.at(l, 1))
                pe.wait_ge(m_root.sem, m_root.at(l, 2))
                for b in range(5):
                    w = P if b < 4 else NS
                    bank = 4 + b % 4
                    if b == 4:
                        pe.wait_ge(tok_ev.sem, tok_ev.at(l, 1))
                    for i in range(4):
                        last = pe.transpose(ps[0:w, bank, i * P:(i + 1) * P], ret_v[:, i, b * P:b * P + w], ident[:, :])
                        if b == 0 and i == 0:
                            last.then_inc(w_used.sem, 1)
                    last.then_inc(tok_mm.sem, 1)
                pe.wait_ge(kv_ready.sem, kv_ready.at(l, 1))
                pe.wait_ge(tok_ev.sem, tok_ev.at(l, 2))
                for b in range(4):
                    last = pe.transpose(ps[:, 5, b * P:(b + 1) * P], kv[:, b * P:(b + 1) * P], ident[:, :])
                last.then_inc(tok_mm.sem, 1)
                pe.wait_ge(tok_ev.sem, tok_ev.at(l, 3))
                pe.transpose(ps[0:NS, 6, 0:P], kv[:, 512:T], ident[:, :]).then_inc(tok_mm.sem, 1)

                pe.wait_ge(rope.sem, rope.at(l, 27))
                pe.wait_ge(uq_ev.sem, uq_ev.at(l, 8))
                pe.wait_ge(tok_ev.sem, tok_ev.at(l, 6))
                for i in range(4):
                    last = pe.transpose(ps[0:NS, 5, i * P:(i + 1) * P], ret_k[:, i, 512:T], ident[:, :])
                last.then_inc(kt_mm.sem, 1)
                for h in range(HEADS):
                    r = slice(32 * (h % 4), 32 * (h % 4) + 32)
                    for half in range(2):
                        i = h // 4 + 2 * half
                        last = pe.matmul(ps[0:NS, h % 4, (h // 4) * NS:(h // 4 + 1) * NS], ret_k[r, i, 512:T], ret_q[r, i, 512:T],
                                         start=half == 0, stop=half == 1)
                last.then_inc(ss_mm.sem, 1)
                pe.wait_ge(tok_ev.sem, tok_ev.at(l, 7))
                pe.wait_ge(ss_mul.sem, ss_mul.at(l, 3))
                pe.wait_ge(tables.sem, tables.at(l, 32))
                for h in range(HEADS):
                    rows = slice(64 * (h % 2), 64 * (h % 2) + 64)
                    dst = ps[rows, 7, (h // 2) * NS:(h // 2 + 1) * NS]
                    pe.matmul(dst, v_tok[0:NS, 4, h * VD:(h + 1) * VD], ret_ss[:, h, :], start=True, stop=False)
                    for half in range(2):
                        i = h // 4 + 2 * half
                        last = pe.matmul(dst, state_in[:, i, :], q_cross[:, i, h % 4, :], start=False, stop=half == 1)
                last.then_inc(so_mm.sem, 1)

                def ret_scores(h):
                    r = slice(32 * (h % 4), 32 * (h % 4) + 32)
                    for b in range(4):
                        if h:
                            pe.wait_ge(rs_mul.sem, rs_mul.at(l, 4 * (h - 1) + b + 1))
                        for half in range(2):
                            i = h // 4 + 2 * half
                            last = pe.matmul(ps[:, b, 0:512 - b * P], ret_k[r, i, b * P:(b + 1) * P],
                                             ret_q[r, i, b * P:512], start=half == 0, stop=half == 1)
                        last.then_inc(rs_mm.sem, 1)

                def state(i):
                    pe.wait_ge(kt_ev.sem, kt_ev.at(l, 2 + i))
                    for b in range(4):
                        last = pe.transpose(ps[:, 4, b * P:(b + 1) * P], ret_k[:, i, b * P:(b + 1) * P], ident[:, :])
                    last.then_inc(kt_mm.sem, 1)

                def state_mm(i):
                    g = i % 2
                    pe.wait_ge(kt_ev.sem, kt_ev.at(l, 3 + i))
                    if i:
                        pe.wait_ge(st_ev.sem, st_ev.at(l, 8 * i))
                    for b in range(4):
                        pe.matmul(ps[:, 5, 0:256], k_tok[:, b, :], v_tok[:, b, g * 256:(g + 1) * 256],
                                  start=b == 0, stop=b == 3)
                    pe.matmul(ps[:, 5, 256:512], k_toks[:, i, :], v_tok[0:NS, 4, g * 256:(g + 1) * 256],
                              start=True, stop=True).then_inc(st_mm.sem, 1)

                ret_scores(0)
                for h in range(HEADS):
                    if h < HEADS - 1:
                        ret_scores(h + 1)
                    if h % 2 == 0:
                        state(h // 2)
                    else:
                        state_mm(h // 2)
                    rows = slice(64 * (h % 2), 64 * (h % 2) + 64)
                    bank = 6 + (h // 2) % 2
                    if h == 2:
                        pe.wait_ge(so_ev.sem, so_ev.at(l, 1))
                    if h >= 4:
                        pe.wait_ge(ro_ev.sem, ro_ev.at(l, h // 2 - 1))
                    for b in range(4):
                        pe.wait_ge(rs_mul.sem, rs_mul.at(l, 4 * h + b + 1))
                        last = pe.matmul(ps[rows, bank, b * P:512], v_tok[:, b, h * VD:(h + 1) * VD],
                                         ret_st[:, b, 0:512 - b * P], start=b == 0, stop=b == 3)
                    last.then_inc(ro_mm.sem, 1)

                pe.wait_ge(st_ev.sem, st_ev.at(l, 32))
                for h in range(HEADS):
                    rows = slice(64 * (h % 2), 64 * (h % 2) + 64)
                    if h >= 2:
                        pe.wait_ge(qa_ev.sem, qa_ev.at(l, h - 1))
                    else:
                        pe.wait_ge(rs_mul.sem, rs_mul.at(l, 32))
                    for t, n in enumerate((slice(0, 512), slice(512, T))):
                        last = pe.matmul(ps[:, 2 * (h % 2) + t, 0:n.stop - n.start], w_ukv[rows, h // 2, :],
                                         q_nope[rows, h // 2, n], start=True, stop=True)
                    last.then_inc(qa_mm.sem, 1)
                    if h % 2:
                        n = h // 2
                        if n >= 2:
                            pe.wait_ge(m_root.sem, m_root.at(l, 2 + n - 1))
                        elif n == 0:
                            pe.wait_ge(st_ev.sem, st_ev.at(l, 32))
                        else:
                            pe.wait_ge(ro_ev.sem, ro_ev.at(l, 4))
                        norm_sum(3 + n, n % 2, 4 + 2 * (n % 2), True, True, half_ones)

                bank_exp = {0: 0, 1: 0, 2: 0, 3: 0}
                def scores(n):
                    kind, h = ITEMS[n]
                    u = FIRST_UNIT[n]
                    if n == 0:
                        pe.wait_ge(rope.sem, rope.at(l, 33))
                    if kind == "p":
                        r = slice(32 * (h % 4), 32 * (h % 4) + 32)
                        for j in range(4):
                            if n == 0:
                                pe.wait_ge(qa_ev.sem, qa_ev.at(l, HEADS))
                            if bank_exp[j]:
                                pe.wait_ge(sc_exp.sem, sc_exp.at(l, bank_exp[j]))
                            q = slice(j * P, (j + 1) * P)
                            w = (j + 1) * P
                            pe.matmul(ps[:, j, 0:w], q_abs[:, h, q], kv[:, 0:w], start=True, stop=False)
                            pe.matmul(ps[0:64, j, w - 64:w], ones[r.start:r.start + 1, 0:64], neg_row[r.start:r.start + 1, :], start=False, stop=False,
                                      skip_group_check=True)
                            pe.matmul(ps[:, j, 0:w], q_pe[r, h // 4, q], kpe[r, 0:w], start=False, stop=True)\
                                .then_inc(sc_mm.sem, 1)
                            bank_exp[j] = u + j + 1
                        return
                    pe.wait_ge(caches.sem, caches.at(l, 48))
                    pe.wait_ge(cache_new.sem, cache_new.at(l, 4))
                    for t in range(2):
                        pe.wait_ge(sc_exp.sem, sc_exp.at(l, bank_exp[t]))
                        k = slice(t * HT, (t + 1) * HT)
                        pe.matmul(ps[:, t, 0:HT], q_abss[:, 4 * h:4 * h + 4, :].rearrange("p h n -> p (h n)"), cache_kv[:, k], start=True, stop=False)
                        last = pe.matmul(ps[:, t, 0:HT], q_pes[:, h, :, :].rearrange("p h n -> p (h n)"), cache_pe[:, k],
                                         start=False, stop=True)
                        bank_exp[t] = u + 1
                    last.then_inc(sc_mm.sem, 1)

                def turned(n):
                    kind, h = ITEMS[n]
                    if n == 0:
                        pe.wait_ge(m_root.sem, m_root.at(l, 6))
                    for j in range(4 if kind == "p" else 1):
                        u = FIRST_UNIT[n] + j
                        if u >= 2:
                            pe.wait_ge(at_ev.sem, at_ev.at(l, u - 1))
                        pe.wait_ge(sc_norm.sem, sc_norm.at(l, 2 * u + 2))
                        blocks = j + 1 if kind == "p" else 4
                        for kb in range(blocks):
                            last = pe.transpose(ps[:, 4 + u % 2, kb * P:(kb + 1) * P],
                                                prob[:, u % 4, kb * P:(kb + 1) * P], ident[:, :])
                        if kind == "s":
                            pe.wait_ge(pv_ev.sem, pv_ev.at(l, n))
                            last = pe.transpose(ps[0:NS, 6, 0:P], prob[:, u % 4, 512:T], ident[:, :])
                        last.then_inc(at_mm.sem, 1)

                def values(n):
                    kind, h = ITEMS[n]
                    if n:
                        pe.wait_ge(pv_ev.sem, pv_ev.at(l, n))
                    units = FIRST_UNIT[n] + (4 if kind == "p" else 1)
                    pe.wait_ge(at_ev.sem, at_ev.at(l, units))
                    if kind == "p":
                        for kb in range(4):
                            last = pe.matmul(ps[:, 6, kb * P:512], kv_tok[:, kb, :], pt[:, n % 2, kb, kb * P:512],
                                             start=kb == 0, stop=kb == 3)
                    else:
                        for kb in range(4):
                            pe.matmul(ps[:, 6, 0:P], cache_tok[:, kb, :], pt[:, n % 2, kb, 0:P], start=kb == 0, stop=False)
                        last = pe.matmul(ps[:, 6, 0:P], kv_tok[0:NS, 4, :], pt[0:NS, n % 2, 0, P:2 * P],
                                         start=False, stop=True)
                    last.then_inc(pv_mm.sem, 1)

                def heads_out(n):
                    kind, h = ITEMS[n]
                    if kind == "s":
                        return
                    pe.wait_ge(pv_ev.sem, pv_ev.at(l, n + 1))
                    rows = slice(64 * (h % 2), 64 * (h % 2) + 64)
                    if h % 2 == 0 and h:
                        pe.wait_ge(uv_lo.sem, uv_lo.at(l, h // 2))
                    last = pe.matmul(ps[rows, 7, :], w_ukv[:, 4 + h // 2, rows], o_lat[:, h % 2, :], start=True, stop=True)
                    if h % 2:
                        last.then_inc(uv_mm.sem, 1)

                scores(0)
                for n in range(len(ITEMS)):
                    if n + 1 < len(ITEMS):
                        scores(n + 1)
                    if n:
                        heads_out(n - 1)
                    turned(n)
                    values(n)
                heads_out(len(ITEMS) - 1)
                for h in range(HEADS):
                    rows = slice(64 * (h % 2), 64 * (h % 2) + 64)
                    last = pe.matmul(ps[rows, 6, (h // 2) * NS:(h // 2 + 1) * NS], w_ukv[:, 4 + h // 2, rows],
                                     o_lats[:, h, :], start=True, stop=True)
                last.then_inc(uv_mm.sem, 1)

                def ready(k):
                    if k == 0:
                        pe.wait_ge(ret_low.sem, ret_low.at(l, 4))
                        pe.wait_ge(at_ev.sem, at_ev.at(l, SU))
                    if k >= 4:
                        pe.wait_ge(uv_lo.sem, uv_lo.at(l, 5))

                def operand(k):
                    return (ret_hi[:, k, :], ret_lo[:, k, :]) if k < 4 else (mla_hi[:, k - 4, :], mla_lo[:, k - 4, :])

                out_tiles(l, 1, MIX_C0 + OUT_C0, 1, KD, operand, ready)

            with pe.Fori(0, DEPTH) as l:
                ffn(l, 0)
                mixer(l)
                ffn(l, 1)

        @block.scalar
        def _(act):
            def used(l, c):
                act.wait_ge(w_used.sem, w_used.at(l, c + 1))

            def high(l, c, slot, width):
                act.wait_ge(w_used.sem, w_used.at(l, c - 1))
                act.wait_ge(landed[slot].sem, landed[slot].at(l, 16 * (c // 2) + 16))
                nc.scalar.copy(w_hi[:, slot, 0:width], raw[:, slot, 0:width]).then_inc(hi_done.sem, 1)

            def high_at(l, base, i2, k, width):
                c = base + 2 * i2 + k
                act.wait_ge(w_used.sem, w_used.at(l, c - 1))
                act.wait_ge(landed[k].sem, landed[k].at(l, 16 * (base // 2) + 16 * i2 + 16))
                nc.scalar.copy(w_hi[:, k, 0:width], raw[:, k, 0:width]).then_inc(hi_done.sem, 1)

            def root_of(l, sig, n, bank, count):
                nc.scalar.activation(halves(root[:, :]), pair(bank), ACT.Sqrt, bias=eps[:, 0:1],
                                     scale=1.0 / count).then_inc(sig.sem, 1)

            def pre_norm(l, j, next_chunk):
                for k in range(2):
                    high(l, next_chunk + k, k, KD * P)
                for m in range(KD):
                    act.wait_ge(x_new.sem, x_new.at(l, (j - 1) * KD + m + 1))
                    act.wait_ge(sums.sem, sums.at(l, 2 * j * KD + m - 1))
                    nc.scalar.activation(tmp_s[:, m % 2, :], x[:, m, :], ACT.Square).then_inc(x_sq.sem, 1)
                act.wait_ge(sums.sem, sums.at(l, 2 * j * KD + KD))
                root_of(l, rooted, 2 * j, 6, D)
                if j:
                    act.wait_ge(columns.sem, columns.at(l, COL_A))
                else:
                    act.wait_ge(columns.sem, columns.at(l, 0))
                for m in range(KD):
                    act.wait_ge(h_scaled.sem, h_scaled.at(l, j * 16 + 2 * m + 2))
                    for v, n in enumerate((slice(0, NP_), slice(NP_, T))):
                        c = 3 * j * KD + m
                        nc.scalar.activation(h_hi[:, m, n], tmp_v[:, m % 2, n], ACT.Identity,
                                             bias=mods[:, v, c:c + 1]).then_inc(h_high.sem, 1)

            def up(l, s):
                base = FFN_C[s]

                def tile(i, f, last_width):
                    n = s * FT + i * 2 + f
                    for k in range(2):
                        high_at(l, base, i * 2 + f + 1, k, last_width if f else KD * P)
                    act.wait_ge(w_used.sem, w_used.at(l, base + i * 4 + 2 * f + 2))
                    nc.scalar.activation(halves(tmp_s[:, f, :]), pair(4 * f), ACT.Silu).then_inc(up_silu.sem, 1)
                    act.wait_ge(up_mul.sem, up_mul.at(l, n + 1))
                    nc.scalar.copy(u_hi[:, bass.ds(i * 2 + f, 1), :].rearrange("p a n -> p (a n)"),
                                   tmp_v[:, f, :]).then_inc(up_hi.sem, 1)

                with act.Fori(0, FT // 2 - 1) as i:
                    tile(i, 0, KD * P)
                    tile(i, 1, KD * P)
                tile(FT // 2 - 1, 0, KD * P)
                tile(FT // 2 - 1, 1, DN_T * P)

            def out_tiles(l, j, chunk0, per_tile, chunk_tiles, o_buf):
                def tile(m, mm, i2):
                    if i2 is not None and per_tile == 2:
                        for k in range(2):
                            high_at(l, chunk0, m + 1, k, chunk_tiles * P)
                    elif i2 is not None:
                        high_at(l, chunk0, i2, mm, chunk_tiles * P)
                    act.wait_ge(w_used.sem, w_used.at(l, chunk0 + (m + 1) * per_tile))
                    o_tile = o_buf[:, bass.ds(m, 1), :].rearrange("p a (t n) -> p (a t) n", t=2)
                    nc.scalar.copy(o_tile, pair(2 * mm)).then_inc(out_ev.sem, 1)
                    act.wait_ge(sums.sem, sums.at(l, (2 * j + 1) * KD + m - 1))
                    nc.scalar.activation(halves(tmp_s[:, mm, :]), pair(2 * mm), ACT.Square).then_inc(out_sq.sem, 1)

                with act.Fori(0, KD // 2 - 1) as i:
                    for mm in range(2):
                        tile(i * 2 + mm, mm, i + 1)
                tile(KD - 2, 0, KD // 2 if per_tile == 2 else None)
                tile(KD - 1, 1, None)
                act.wait_ge(sums.sem, sums.at(l, (2 * j + 2) * KD))
                root_of(l, rooted, 2 * j + 1, 4, D)

            def ffn(l, s):
                pre_norm(l, 2 * s, FFN_C[s])
                up(l, s)
                out_tiles(l, 2 * s, FFN_C[s] + UP_C, 2, DN_T, o_ffn)

            def mixer(l):
                pre_norm(l, 1, MIX_C0)

                def z_out(z, bank, dst, func=ACT.Copy):
                    act.wait_ge(w_used.sem, w_used.at(l, MIX_C0 + z + 1))
                    nc.scalar.activation(dst, pair(bank), func).then_inc(z_ev.sem, 1)

                def square(n, buf, src):
                    nc.scalar.activation(tmp_s[:, buf, :], src, ACT.Square).then_inc(m_sq.sem, 1)

                early = [zq[:, 0, :], zq[:, 1, :], kv[:, :], kpe[:, :], kpe_swap[:, :]]
                for z in range(Z_EARLY):
                    high(l, MIX_C0 + z + 2, z % 2, KD * P)
                    z_out(z, 2 * (z % 2), halves(early[z]))
                    if z < 3:
                        act.wait_ge(z_ev.sem, z_ev.at(l, z + 1))
                        if z == 2:
                            act.wait_ge(m_sum.sem, m_sum.at(l, 1))
                        square(z, z % 2, early[z])
                    if z == 3:
                        act.wait_ge(m_sum.sem, m_sum.at(l, 2))
                        root_of(l, m_root, 0, 4, Q_RANK)
                    if z == 4:
                        act.wait_ge(m_sum.sem, m_sum.at(l, 3))
                        act.wait_ge(m_inv.sem, m_inv.at(l, 1))
                        root_of(l, m_root, 1, 6, KV_RANK)
                        for k in range(2):
                            act.wait_ge(q_scaled.sem, q_scaled.at(l, k + 1))
                            nc.scalar.copy(qn_hi[:, k, :], tmp_v[:, k, :]).then_inc(q_high.sem, 1)
                with act.Fori(0, 4) as i:
                    for t, dst in enumerate((ret_q, ret_k, ret_v, ret_g)):
                        z = Z_EARLY + t
                        c = MIX_C0 + z + 2
                        act.wait_ge(w_used.sem, w_used.at(l, i * 4 + c - 1))
                        act.wait_ge(landed[z % 2].sem, landed[z % 2].at(l, i * 32 + 16 * (c // 2) + 16))
                        nc.scalar.copy(w_hi[:, z % 2, 0:KD * P], raw[:, z % 2, 0:KD * P]).then_inc(hi_done.sem, 1)
                        z_out(i * 4 + z, 2 * (z % 2),
                              dst[:, bass.ds(i, 1), :].rearrange("p a (t n) -> p (a t) n", t=2),
                              ACT.Silu if t == 3 else ACT.Copy)
                act.wait_ge(landed[(Z_C + UQ_C) % 2].sem, landed[(Z_C + UQ_C) % 2].at(l, 16 * ((MIX_C0 + Z_C + UQ_C) // 2) + 16))
                nc.scalar.copy(w_ukv[:, :, :].rearrange("p a n -> p (a n)"),
                               raw[:, (Z_C + UQ_C) % 2, 0:KD * P]).then_inc(ukv_in.sem, 1)
                uq_dst = [q_nope[:, n, :] for n in range(4)] + [q_pe[:, n, :] for n in range(2)] + \
                         [q_pe_swap[:, n, :] for n in range(2)]
                for n in range(8):
                    if n == 4:
                        high(l, MIX_C0 + Z_C + UQ_C, (Z_C + UQ_C) % 2, KD * P)
                    if n % 4 == 3:
                        used(l, MIX_C0 + Z_C + n // 4)
                    else:
                        act.wait_ge(uq_mm.sem, uq_mm.at(l, n - n // 4 + 1))
                    nc.scalar.copy(halves(uq_dst[n]), pair(2 * (n % 2))).then_inc(uq_ev.sem, 1)
                high(l, MIX_C0 + OUT_C0, OUT_C0 % 2, KD * P)
                for n in range(7):
                    act.wait_ge(tok_mm.sem, tok_mm.at(l, n + 1))
                    if n < 5:
                        w = P if n < 4 else NS
                        nc.scalar.copy(v_tok[0:w, n, :], ps[0:w, 4 + n % 4, :])\
                            .then_inc(tok_ev.sem, 1)
                    elif n == 5:
                        nc.scalar.copy(kv_tok[:, 0:4, :].rearrange("p a n -> p (a n)"), ps[:, 5, :]).then_inc(tok_ev.sem, 1)
                    else:
                        nc.scalar.copy(kv_tok[0:NS, 4, :], ps[0:NS, 6, 0:P]).then_inc(tok_ev.sem, 1)
                high(l, MIX_C0 + OUT_C0 + 1, 1, KD * P)
                act.wait_ge(so_mm.sem, so_mm.at(l, 1))
                nc.scalar.copy(ret_v[:, :, 512:T], ps[:, 7, 0:4 * NS].rearrange("p (a n) -> p a n", a=4))\
                    .then_inc(so_ev.sem, 1)
                for n in range(4):
                    act.wait_ge(ro_mm.sem, ro_mm.at(l, 2 * n + 2))
                    nc.scalar.copy(ret_v[:, n, 0:512], ps[:, 6 + n % 2, :]).then_inc(ro_ev.sem, 1)

                def norm_square(n):
                    act.wait_ge(ro_ev.sem, ro_ev.at(l, n + 1))
                    act.wait_ge(m_sum.sem, m_sum.at(l, 3 + n - 1))
                    square(3 + n, n % 2, ret_v[:, n, :])

                def norm_root(n):
                    act.wait_ge(m_sum.sem, m_sum.at(l, 3 + n + 1))
                    act.wait_ge(m_inv.sem, m_inv.at(l, 2 + n))
                    root_of(l, m_root, 2 + n, 4 + 2 * (n % 2), VD)

                act.wait_ge(so_ev.sem, so_ev.at(l, 1))
                norm_square(0)
                norm_square(1)
                for h in range(HEADS):
                    act.wait_ge(qa_mm.sem, qa_mm.at(l, h + 1))
                    nc.scalar.copy(q_abss[:, h, :], ps[:, 2 * (h % 2) + 1, 0:NS])
                    nc.scalar.copy(q_abs[:, h, :], ps[:, 2 * (h % 2), :]).then_inc(qa_ev.sem, 1)
                    if h in (1, 3, 5, 7):
                        norm_root(h // 2)
                        if h // 2 + 2 < 4:
                            norm_square(h // 2 + 2)
                    if h in (3, 5, 7):
                        ret_out(l, h // 2 - 1)
                ret_out(l, 3)

                def exponential(n, j):
                    kind, h = ITEMS[n]
                    u = FIRST_UNIT[n] + j
                    act.wait_ge(sc_max.sem, sc_max.at(l, 2 * u + 2))
                    if u >= 4:
                        act.wait_ge(at_mm.sem, at_mm.at(l, u - 3))
                    if kind == "p":
                        w = (j + 1) * P
                        src, dst = ps[:, j, 0:w], prob[:, u % 4, 0:w]
                    else:
                        src, dst = pair(0), halves(prob[:, u % 4, :])
                    c = slice(u % 4, u % 4 + 1)
                    nc.scalar.activation(dst, src, ACT.Exp, bias=neg_max[:, c], scale=MLA_SCALE,
                                         accum_out=exp_sum[:, c]).then_inc(sc_exp.sem, 1)

                def turned(n, j):
                    kind, h = ITEMS[n]
                    u = FIRST_UNIT[n] + j
                    act.wait_ge(at_mm.sem, at_mm.at(l, u + 1))
                    if n >= 2 and j == 0:
                        act.wait_ge(pv_mm.sem, pv_mm.at(l, n - 1))
                    if kind == "p":
                        nc.scalar.copy(pt[:, n % 2, 0:j + 1, j * P:(j + 1) * P],
                                       ps[:, 4 + u % 2, 0:(j + 1) * P].rearrange("p (a n) -> p a n", a=j + 1))\
                            .then_inc(at_ev.sem, 1)
                    else:
                        nc.scalar.copy(pt[0:NS, n % 2, 0, P:2 * P], ps[0:NS, 6, 0:P])
                        nc.scalar.copy(pt[:, n % 2, 0:4, 0:P],
                                       ps[:, 4 + u % 2, :].rearrange("p (a n) -> p a n", a=4)).then_inc(at_ev.sem, 1)

                units = [4 if kind == "p" else 1 for kind, _ in ITEMS] + [0]
                for j in range(4):
                    exponential(0, j)
                for n in range(len(ITEMS)):
                    for j in range(max(units[n], units[n + 1])):
                        if j < units[n]:
                            turned(n, j)
                        if j < units[n + 1]:
                            exponential(n + 1, j)
                    if n and ITEMS[n - 1][0] == "p" and ITEMS[n - 1][1] % 2:
                        heads_high(l, ITEMS[n - 1][1] // 2)
                heads_high(l, 3)
                act.wait_ge(uv_mm.sem, uv_mm.at(l, 5))
                nc.scalar.copy(mla_hi[:, :, 512:T], ps[:, 6, 0:4 * NS].rearrange("p (a n) -> p a n", a=4))\
                    .then_inc(uv_hi.sem, 1)
                act.wait_ge(stored.sem, stored.at(l, 64))
                out_tiles(l, 1, MIX_C0 + OUT_C0, 1, KD, o_mix)

            def ret_out(l, n):
                act.wait_ge(ret_prod.sem, ret_prod.at(l, 2 * n + 2))
                nc.scalar.copy(ret_hi[:, n, :], tmp_v[:, n % 2, :]).then_inc(ret_high.sem, 1)

            def heads_high(l, p):
                act.wait_ge(uv_mm.sem, uv_mm.at(l, p + 1))
                nc.scalar.copy(mla_hi[:, p, 0:512], ps[:, 7, :]).then_inc(uv_hi.sem, 1)

            act.wait_ge(filled.sem, 3)
            act.wait_ge(c_in.sem, 16)
            nc.scalar.activation(c_all[:, :, :], c_all[:, :, :], ACT.Silu).then_inc(c_act.sem, 1)
            with act.Fori(0, DEPTH) as l:
                ffn(l, 0)
                mixer(l)
                ffn(l, 1)

        @block.vector
        def _(dve):
            v_ = nc.vector
            GROUPS = (slice(0, NP_), slice(NP_, T))

            v_.memset(ones[:, :], 1.0).then_inc(filled.sem, 1)
            v_.memset(eps[:, :], EPS).then_inc(filled.sem, 1)
            v_.memset(neg_row[:, :], NEG).then_inc(filled.sem, 1)
            for k in range(2):
                v_.memset(scratch[:, 2 + k:3 + k], 0.0).then_inc(up_mul.sem, 1)
                v_.memset(scratch[:, 12 + k:13 + k], 0.0).then_inc(up_lo.sem, 1)

            def ada_group(l, land_n, n0, done0, cols, before_group=0, first_ffn=False):
                for t in range(ADA_RING):
                    if before_group is None:
                        dve.wait_ge(ada_landed[t].sem, 16 * (land_n + 1))
                    else:
                        dve.wait_ge(ada_landed[t].sem, ada_landed[t].at(l, land_n * 16 + 16))
                    if t == 0 and before_group is None:
                        if cols:
                            dve.wait_ge(columns.sem, cols)
                    elif t == 0:
                        dve.wait_ge(columns.sem, columns.at(l, cols))
                        dve.wait_ge(up_lo.sem, up_lo.at(l, FT if first_ffn else 2 * FT))
                    for v in range(2):
                        if before_group is None:
                            if done0 or t:
                                dve.wait_ge(ada_done.sem, 2 * (done0 + t) + v - 1)
                        else:
                            dve.wait_ge(ada_done.sem, ada_done.at(l, 2 * done0 + (2 * t + v - 1)))
                        v_.tensor_tensor_reduce(junk[v], ada_w[:, t, :], c_all[:, v, :], 1.0, 0.0, ALU.mult,
                                                ALU.add, acc[:, v, t:t + 1]).then_inc(ada_done.sem, 1)
                if before_group is None:
                    dve.wait_ge(ada_done.sem, 2 * (done0 + ADA_RING))
                else:
                    dve.wait_ge(ada_done.sem, ada_done.at(l, 2 * done0 + 2 * ADA_RING))
                for v in range(2):
                    bias = ada_b[:, bass.ds(before_col(l, before_group, done0), ADA_RING)]
                    v_.tensor_tensor(mods[:, v, bass.ds(n0, ADA_RING)], acc[:, v, :], bias, ALU.add)\
                        .then_inc(columns.sem, 1)

            def before_col(l, before_group, done0):
                return done0 if before_group is None else l * MODS + 16 + done0

            def pre_columns(l, j, layer_of):
                for v in range(2):
                    c = (3 * j + 1) * KD
                    v_.scalar_tensor_tensor(out=mul_pre[:, j, v, :], in0=mods[:, v, c:c + KD], scalar=1.0,
                                            in1=g_pre[:, bass.ds(layer_of * 3 * KD + j * KD, KD)],
                                            op0=ALU.add, op1=ALU.mult).then_inc(columns.sem, 1)

            def post_columns(l, j):
                for v in range(2):
                    c = (3 * j + 2) * KD
                    v_.scalar_tensor_tensor(out=mul_post[:, j, v, :], in0=mods[:, v, c:c + KD],
                                            scalar=1.0 if j == 1 else 0.5,
                                            in1=g_post[:, bass.ds(l * 3 * KD + j * KD, KD)],
                                            op0=ALU.mult, op1=ALU.mult).then_inc(columns.sem, 1)

            def invert(l, root_sig, inv_sig, n):
                dve.wait_ge(root_sig.sem, root_sig.at(l, n + 1))
                v_.reciprocal(rinv[:, :], root[:, :]).then_inc(inv_sig.sem, 1)
                dve.wait_ge(inv_sig.sem, inv_sig.at(l, n + 1))

            def pre_norm(l, j):
                invert(l, rooted, inverted, 2 * j)
                dve.wait_ge(columns.sem, columns.at(l, COL_A if j else 0))

                def low(m):
                    dve.wait_ge(h_high.sem, h_high.at(l, j * 16 + 2 * m + 2))
                    for v, n in enumerate(GROUPS):
                        c = 3 * j * KD + m
                        v_.scalar_tensor_tensor(out=h_lo[:, m, n], in0=tmp_v[:, m % 2, n], scalar=mods[:, v, c:c + 1],
                                                in1=h_hi[:, m, n].bitcast(F32), op0=ALU.add, op1=ALU.subtract)\
                            .then_inc(h_ready.sem, 1)

                for m in range(KD):
                    if m >= 2:
                        dve.wait_ge(h_ready.sem, h_ready.at(l, j * 16 + 2 * m - 2))
                    for v, n in enumerate(GROUPS):
                        v_.scalar_tensor_tensor(out=tmp_v[:, m % 2, n], in0=x[:, m, n], scalar=mul_pre[:, j, v, m:m + 1],
                                                in1=rinv[:, n], op0=ALU.mult, op1=ALU.mult).then_inc(h_scaled.sem, 1)
                    if m:
                        low(m - 1)
                low(KD - 1)

            def post_norm(l, j, o_buf):
                invert(l, rooted, inverted, 2 * j + 1)
                dve.wait_ge(columns.sem, columns.at(l, COL_A + (COL_B if j == 2 else 0)))

                def add(m):
                    dve.wait_ge(x_prod.sem, x_prod.at(l, j * 16 + 2 * m + 2))
                    v_.tensor_tensor(x[:, m, :], x[:, m, :], tmp_v[:, m % 2, :], ALU.add).then_inc(x_new.sem, 1)

                for m in range(KD):
                    if m >= 2:
                        dve.wait_ge(x_new.sem, x_new.at(l, j * KD + m - 1))
                    for v, n in enumerate(GROUPS):
                        v_.scalar_tensor_tensor(out=tmp_v[:, m % 2, n], in0=o_buf[:, m, n], scalar=mul_post[:, j, v, m:m + 1],
                                                in1=rinv[:, n], op0=ALU.mult, op1=ALU.mult).then_inc(x_prod.sem, 1)
                    if m:
                        add(m - 1)
                add(KD - 1)

            def ffn(l, s):
                pre_norm(l, 2 * s)
                with dve.Fori(0, FT // 2) as i:
                    for f in range(2):
                        n = s * FT + i * 2 + f
                        dve.wait_ge(up_lo.sem, up_lo.at(l, n - 1))
                        dve.wait_ge(up_silu.sem, up_silu.at(l, n + 1))
                        v_.tensor_tensor(halves(tmp_v[:, f, :]), halves(tmp_s[:, f, :]), pair(4 * f + 2), ALU.mult)\
                            .then_inc(up_mul.sem, 1)
                        dve.wait_ge(up_hi.sem, up_hi.at(l, n + 1))
                        at = bass.ds(i * 2 + f, 1)
                        v_.tensor_tensor(u_lo[:, at, :].rearrange("p a n -> p (a n)"), tmp_v[:, f, :],
                                         u_hi[:, at, :].rearrange("p a n -> p (a n)").bitcast(F32), ALU.subtract)\
                            .then_inc(up_lo.sem, 1)
                if s == 0:
                    with dve.Fori(0, ADA_A // ADA_RING) as i:
                        ada_group(l, i, 16 + i * ADA_RING, i * ADA_RING, i * 2, first_ffn=True)
                    dve.wait_ge(columns.sem, columns.at(l, 2 * ADA_A // ADA_RING))
                    post_columns(l, 0)
                    pre_columns(l, 1, l)
                    post_columns(l, 1)
                    pre_columns(l, 2, l)
                else:
                    g0 = ADA_A // ADA_RING
                    with dve.Fori(0, 2) as i:
                        ada_group(l, i + g0, 64 + i * ADA_RING, ADA_A + i * ADA_RING, i * 2 + COL_A)
                    with dve.Fori(0, 4) as i:
                        ada_group(l, i + (g0 + 2), i * ADA_RING, (ADA_A + 8) + i * ADA_RING, i * 2 + (COL_A + 4))
                    dve.wait_ge(columns.sem, columns.at(l, COL_A + 2 * ADA_B // ADA_RING))
                    post_columns(l, 2)
                    pre_columns(l, 0, l + 1)
                post_norm(l, 2 * s, o_ffn)

            def mixer(l):
                pre_norm(l, 1)
                v_.tensor_copy(gains[:, :], g_lat[:, bass.ds(l * 3, 3)]).then_inc(gains_in.sem, 1)
                dve.wait_ge(gains_in.sem, gains_in.at(l, 1))
                invert(l, m_root, m_inv, 0)
                for k in range(2):
                    v_.scalar_tensor_tensor(out=tmp_v[:, k, :], in0=zq[:, k, :], scalar=gains[:, k:k + 1], in1=rinv[:, :],
                                            op0=ALU.mult, op1=ALU.mult).then_inc(q_scaled.sem, 1)
                dve.wait_ge(q_scaled.sem, q_scaled.at(l, 2))
                invert(l, m_root, m_inv, 1)
                v_.scalar_tensor_tensor(out=kv[:, :], in0=kv[:, :], scalar=gains[:, 2:3], in1=rinv[:, :],
                                        op0=ALU.mult, op1=ALU.mult).then_inc(kv_ready.sem, 1)
                for k in range(2):
                    dve.wait_ge(q_high.sem, q_high.at(l, k + 1))
                    v_.tensor_tensor(qn_lo[:, k, :], tmp_v[:, k, :], qn_hi[:, k, :].bitcast(F32), ALU.subtract)\
                        .then_inc(q_low.sem, 1)

                turns = [0]

                def turn(out, in0, in1, op):
                    v_.tensor_tensor(out, in0, in1, op).then_inc(rope.sem, 1)
                    turns[0] += 1

                def turned_so_far():
                    dve.wait_ge(rope.sem, rope.at(l, turns[0]))

                def rotate(t, swapped):
                    turn(tmp_v[:, 0, :], t, rope_tab[:, 2, :], ALU.mult)
                    turn(tmp_v[:, 1, :], swapped, rope_tab[:, 3, :], ALU.mult)
                    turned_so_far()
                    turn(t, tmp_v[:, 0, :], tmp_v[:, 1, :], ALU.add)

                dve.wait_ge(q_low.sem, q_low.at(l, 2))
                dve.wait_ge(tables.sem, tables.at(l, 32))
                dve.wait_ge(z_ev.sem, z_ev.at(l, Z_EARLY))
                rotate(kpe[:, :], kpe_swap[:, :])
                dve.wait_ge(z_ev.sem, z_ev.at(l, Z_C))
                for t in (ret_q, ret_k):
                    for i in range(2):
                        a1, a2 = t[:, i, :], t[:, i + 2, :]
                        cos, sin = rope_tab[:, 0, :], rope_tab[:, 1, :]
                        turned_so_far()
                        turn(tmp_s[:, 0, :], a1, cos, ALU.mult)
                        turn(tmp_s[:, 1, :], a2, sin, ALU.mult)
                        turn(tmp_v[:, 0, :], a1, sin, ALU.mult)
                        turn(tmp_v[:, 1, :], a2, cos, ALU.mult)
                        turned_so_far()
                        turn(a1, tmp_s[:, 0, :], tmp_s[:, 1, :], ALU.subtract)
                        turn(a2, tmp_v[:, 1, :], tmp_v[:, 0, :], ALU.add)
                dve.wait_ge(uq_ev.sem, uq_ev.at(l, 8))
                for g in range(2):
                    turned_so_far()
                    rotate(q_pe[:, g, :], q_pe_swap[:, g, :])

                for half in range(2):
                    v_.tensor_tensor(q_cross[:, 2 * half:2 * half + 2, :, :],
                                     ret_q[:, 2 * half:2 * half + 2, 512:T].unsqueeze(2).to_broadcast([P, 2, 4, NS]),
                                     cross[:, :, :, :], ALU.mult).then_inc(ss_mul.sem, 1)
                dve.wait_ge(ss_mm.sem, ss_mm.at(l, 1))
                dve.wait_ge(decay_in.sem, decay_in.at(l, 16))
                v_.tensor_tensor(ret_ss[:, :, :].rearrange("p (i g) n -> p g i n", g=4),
                                 ps[0:NS, 0:4, 0:2 * NS].rearrange("p g (i n) -> p g i n", i=2),
                                 decay[0:NS, :, 0:NS].rearrange("p (i g) n -> p g i n", g=4), ALU.mult)\
                    .then_inc(ss_mul.sem, 1)
                dve.wait_ge(kt_mm.sem, kt_mm.at(l, 1))
                for half in range(2):
                    v_.tensor_tensor(
                        k_toks[:, 2 * half:2 * half + 2, :].rearrange("p g (h d) -> p (g h) d", h=4),
                        ps[0:NS, 5, 256 * half:256 * half + 256].rearrange("p (g d) -> p g d", g=8),
                        k_decays[:, :].unsqueeze(2).to_broadcast([NS, 8, 32]), ALU.mult).then_inc(kt_ev.sem, 1)
                for h in range(HEADS):
                    if h:
                        dve.wait_ge(ro_mm.sem, ro_mm.at(l, h))
                    for b in range(4):
                        dve.wait_ge(rs_mm.sem, rs_mm.at(l, 4 * h + b + 1))
                        w = 512 - b * P
                        v_.tensor_tensor(ret_st[:, b, 0:w], ps[:, b, 0:w], decay[:, h, 0:w], ALU.mult)\
                            .then_inc(rs_mul.sem, 1)
                    i, g = h // 2, (h // 2) % 2
                    if h % 2 == 0:
                        dve.wait_ge(kt_mm.sem, kt_mm.at(l, 2 + i))
                        if i:
                            dve.wait_ge(st_mm.sem, st_mm.at(l, i))
                        v_.tensor_tensor(k_tok[:, :, :].rearrange("p b (h d) -> p b h d", h=4),
                                         ps[:, 4, :].rearrange("p (b h d) -> p b h d", b=4, h=4),
                                         k_decay[:, g, :, :].unsqueeze(3).to_broadcast([P, 4, 4, 32]), ALU.mult)\
                            .then_inc(kt_ev.sem, 1)
                    else:
                        dve.wait_ge(st_mm.sem, st_mm.at(l, i + 1))
                        for hh in range(4):
                            r = slice(32 * hh, 32 * hh + 32)
                            v_.tensor_copy(state_p[r, i, :], ps[r, 5, hh * VD:(hh + 1) * VD]).then_inc(st_ev.sem, 1)
                            v_.scalar_tensor_tensor(out=state_in[r, i, :], in0=state_in[r, i, :],
                                                    scalar=state_decay[r, g:g + 1],
                                                    in1=ps[r, 5, 256 + hh * VD:256 + (hh + 1) * VD],
                                                    op0=ALU.mult, op1=ALU.add).then_inc(st_ev.sem, 1)

                dve.wait_ge(ro_mm.sem, ro_mm.at(l, HEADS))
                v_.tensor_copy(cache_kv[:, PAST:T], kv[:, 512:T]).then_inc(cache_new.sem, 1)
                v_.tensor_copy(cache_pe[:, PAST:T], kpe[:, 512:T]).then_inc(cache_new.sem, 1)
                dve.wait_ge(rope.sem, rope.at(l, 33))
                for g in range(2):
                    v_.tensor_tensor(q_pes[:, g, :, :], q_pe[:, g, 512:T].unsqueeze(1).to_broadcast([P, 4, NS]),
                                     own_head[:, :, :], ALU.mult).then_inc(cache_new.sem, 1)

                def ret_prods(n):
                    invert(l, m_root, m_inv, 2 + n)
                    if n >= 2:
                        dve.wait_ge(ret_low.sem, ret_low.at(l, n - 1))
                    elif n == 0:
                        dve.wait_ge(rope.sem, rope.at(l, 33))
                    v_.tensor_tensor(tmp_v[:, n % 2, :], ret_v[:, n, :], rinv[:, :], ALU.mult).then_inc(ret_prod.sem, 1)
                    dve.wait_ge(ret_prod.sem, ret_prod.at(l, 2 * n + 1))
                    v_.tensor_tensor(tmp_v[:, n % 2, :], tmp_v[:, n % 2, :], ret_g[:, n, :], ALU.mult)\
                        .then_inc(ret_prod.sem, 1)

                def ret_lows(n):
                    dve.wait_ge(ret_high.sem, ret_high.at(l, n + 1))
                    v_.tensor_tensor(ret_lo[:, n, :], tmp_v[:, n % 2, :], ret_hi[:, n, :].bitcast(F32), ALU.subtract)\
                        .then_inc(ret_low.sem, 1)

                ret_prods(0)
                ret_prods(1)
                for n in (2, 3):
                    ret_lows(n - 2)
                    ret_prods(n)
                ret_lows(2)
                ret_lows(3)

                def maximum(n, j):
                    kind, h = ITEMS[n]
                    u = FIRST_UNIT[n] + j
                    c = slice(u % 4, u % 4 + 1)
                    dve.wait_ge(sc_mm.sem, sc_mm.at(l, u + 1))
                    if kind == "p":
                        v_.reduce_max(row_max[:, c], ps[:, j, 0:(j + 1) * P], AX.X).then_inc(sc_max.sem, 1)
                    else:
                        v_.tensor_reduce(row_max[:, c], pair(0), AX.XY, ALU.max).then_inc(sc_max.sem, 1)
                    dve.wait_ge(sc_max.sem, sc_max.at(l, 2 * u + 1))
                    v_.tensor_scalar(neg_max[:, c], row_max[:, c], -MLA_SCALE, None, ALU.mult).then_inc(sc_max.sem, 1)

                def normal(u):
                    n = max(i for i in range(len(ITEMS)) if FIRST_UNIT[i] <= u)
                    w = (u - FIRST_UNIT[n] + 1) * P if ITEMS[n][0] == "p" else T
                    c = slice(u % 4, u % 4 + 1)
                    dve.wait_ge(sc_exp.sem, sc_exp.at(l, u + 1))
                    v_.reciprocal(inv_sum[:, c], exp_sum[:, c]).then_inc(sc_norm.sem, 1)
                    dve.wait_ge(sc_norm.sem, sc_norm.at(l, 2 * u + 1))
                    v_.tensor_scalar(prob[:, u % 4, 0:w], prob[:, u % 4, 0:w], inv_sum[:, c], None, ALU.mult)\
                        .then_inc(sc_norm.sem, 1)

                def latents_out(n):
                    kind, h = ITEMS[n]
                    dve.wait_ge(pv_mm.sem, pv_mm.at(l, n + 1))
                    if kind == "p":
                        v_.tensor_copy(o_lat[:, h % 2, :], ps[:, 6, :]).then_inc(pv_ev.sem, 1)
                    else:
                        v_.tensor_copy(o_lats[:, 4 * h:4 * h + 4, :], ps[:, 6, 0:P].rearrange("p (h n) -> p h n", h=4))\
                            .then_inc(pv_ev.sem, 1)

                def heads_low(p):
                    dve.wait_ge(uv_hi.sem, uv_hi.at(l, p + 1))
                    v_.tensor_tensor(mla_lo[:, p, 0:512], ps[:, 7, :], mla_hi[:, p, 0:512].bitcast(F32), ALU.subtract)\
                        .then_inc(uv_lo.sem, 1)

                for n in range(len(ITEMS)):
                    for j in range(4 if ITEMS[n][0] == "p" else 1):
                        maximum(n, j)
                        if FIRST_UNIT[n] + j:
                            normal(FIRST_UNIT[n] + j - 1)
                        if j == 0 and n:
                            if n >= 2:
                                latents_out(n - 2)
                            if n >= 3 and ITEMS[n - 3][0] == "p" and ITEMS[n - 3][1] % 2:
                                heads_low(ITEMS[n - 3][1] // 2)
                normal(SU - 1)
                latents_out(len(ITEMS) - 2)
                latents_out(len(ITEMS) - 1)
                heads_low(3)
                dve.wait_ge(uv_hi.sem, uv_hi.at(l, 5))
                v_.tensor_tensor(mla_lo[:, :, 512:T], ps[:, 6, 0:4 * NS].rearrange("p (a n) -> p a n", a=4),
                                 mla_hi[:, :, 512:T].bitcast(F32), ALU.subtract).then_inc(uv_lo.sem, 1)
                post_norm(l, 1, o_mix)

            dve.wait_ge(c_act.sem, 1)
            dve.wait_ge(const_in.sem, 16 * N_CONST)
            for i in range(4):
                ada_group(0, i, i * ADA_RING, i * ADA_RING, 2 * i, None)
            dve.wait_ge(columns.sem, 8)
            pre_columns(0, 0, 0)
            dve.wait_ge(x_in.sem, 16)
            for k in range(KD):
                v_.memset(scratch[:, 4 + k:5 + k], 0.0).then_inc(x_new.sem, 1)
            with dve.Fori(0, DEPTH) as l:
                ffn(l, 0)
                mixer(l)
                ffn(l, 1)


OUTS = {"y": (P, KD, T), "kv": (DEPTH, P, T), "kpe": (DEPTH, ROPE, T),
        "state_p": (DEPTH, P, 4, VD), "state_s": (DEPTH, P, 4, VD)}


def tables():
    pos = np.arange(T, dtype=np.float32)
    p = np.arange(P)

    def angles(half, i):
        inv = np.float32(10000.0) ** (-np.arange(half, dtype=np.float32) / np.float32(half))
        return inv.astype(np.float32)[i][:, None] * pos[None, :]

    ret, mla = angles(32, p % 32), angles(16, p % 16)
    sign = np.where(p % 32 < 16, -1.0, 1.0)[:, None]
    rope = np.stack([np.cos(ret), np.sin(ret), np.cos(mla), sign * np.sin(mla)], 1).astype(np.float32)
    log_g = np.log1p(-np.exp2(-5.0 - np.arange(HEADS)))
    j = np.arange(512)
    diff = j[None, None, :] - p[:, None, None]
    decay = np.where(diff >= 0, np.exp(np.maximum(diff, 0) * log_g[None, :, None]), 0.0) * RET_SCALE
    head = np.arange(HEADS).reshape(2, 4)
    tok = (np.arange(4)[None, :] * P + p[:, None])
    k_decay = np.exp((511 - tok)[:, None, :, None] * log_g[head][None, :, None, :]) * RET_SCALE
    k_decays = np.exp((NS - 1 - np.arange(NS))[:, None] * log_g[None, :]) * RET_SCALE
    of_row = head[:, p // 32].T
    cross = np.exp((np.arange(NS) + 1.0)[None, None, :] * log_g[of_row][:, :, None])
    own = (p[:, None] // 32 == np.arange(4))[:, :, None]
    cross = np.where(own[:, None], cross[:, :, None, :], 0.0)
    state_decay = np.exp(NS * log_g[of_row])
    same = (p[:, None] // VD == p[None, :] // VD)
    return {"rope": rope, "decay": decay, "k_decay": k_decay, "k_decays": k_decays, "cross": cross,
            "state_decay": state_decay, "half_ones": same, "own_head": np.broadcast_to(own, (P, 4, NS)), "ident": np.eye(P)}


def tiles(w, n_k, n_c):
    w = w.reshape(*w.shape[:-2], n_k, P, n_c, P)
    return np.moveaxis(w, -2, -4).swapaxes(-2, -3)


def kernel(**inputs):
    import concourse.bacc as _bacc
    from concourse.bass_utils import run_bass_kernel_spmd as _run

    f = {k: np.asarray(v) for k, v in inputs.items()}
    L = DEPTH

    def feature_major(t):
        return t.T.reshape(KD, P, T).transpose(1, 0, 2)

    a = {k: np.ascontiguousarray(v, dtype=np.float32) for k, v in tables().items()}
    a["x"] = feature_major(np.concatenate([f["x_prompt"][0], f["x_sample"][0]], 0))
    a["c"] = np.stack([f["c_prompt"][0], f["c_sample"][0]])

    ada = f["ada_w"].transpose(0, 2, 1).reshape(L * MODS, P, D)
    a["ada"] = np.concatenate([ada, ada[:16]], 0)
    bias = f["ada_b"].reshape(L * MODS, P)
    a["ada_b"] = np.concatenate([bias, bias[:16]], 0).T
    pre = f["norm_pre"].reshape(L * 3 * KD, P)
    a["g_pre"] = np.concatenate([pre, pre[:KD]], 0).T
    a["g_post"] = f["norm_post"].reshape(L * 3 * KD, P).T
    a["g_lat"] = np.concatenate([f["q_norm"].reshape(L, 2, P), f["kv_norm"].reshape(L, 1, P)], 1).reshape(L * 3, P).T

    w1, w3 = (tiles(f[n], KD, FT) for n in ("ffn_w1", "ffn_w3"))
    a["w_up"] = np.stack([w1, w3], 3).reshape(L * 2 * UP_C, P, KD * P)
    w2 = tiles(f["ffn_w2"], FT, KD)
    w2 = w2.reshape(L, 2, KD, P, 2, DN_T * P).transpose(0, 1, 2, 4, 3, 5)
    a["w_dn"] = w2.reshape(L * 2 * DN_C, P, DN_T * P)

    q0, kv0, pe0, r0 = 0, Q_RANK, Q_RANK + KV_RANK, Q_RANK + KV_RANK + ROPE
    swap = np.r_[ROPE // 2:ROPE, 0:ROPE // 2]
    cols = [np.arange(q0, pe0), np.tile(pe0 + np.arange(ROPE), 4), np.tile(pe0 + swap, 4)]
    n_ret = HEADS * RDK
    halves_first = np.concatenate([
        (np.arange(HEADS)[:, None] * RDK + s * 32 + np.arange(32)[None, :]).ravel() for s in range(2)])
    parts = [r0 + halves_first, r0 + n_ret + halves_first, r0 + 2 * n_ret + np.arange(n_ret),
             r0 + 3 * n_ret + np.arange(n_ret)]
    for i in range(4):
        cols += [part[i * P:(i + 1) * P] for part in parts]
    w_in = tiles(f["w_in"][:, :, np.concatenate(cols)], KD, Z_C).reshape(L, Z_C, P, KD * P)
    per = NOPE + ROPE
    heads = np.arange(HEADS)[:, None] * per
    uq_cols = np.concatenate([(heads + np.arange(NOPE)).ravel(), (heads + NOPE + np.arange(ROPE)).ravel(),
                              (heads + NOPE + swap).ravel()])
    uq = tiles(f["w_uq"][:, :, uq_cols], 2, 8)
    uq = uq.reshape(L, 2, 4, P, 2 * P).transpose(0, 1, 3, 2, 4).reshape(L, 2, P, KD * P)
    uk = f["w_uk"].transpose(0, 2, 1).reshape(L, 4, P, P).transpose(0, 2, 1, 3).reshape(L, P, 4 * P)
    ukv = np.concatenate([uk, f["w_uv"]], 2)[:, None]
    n_mla = HEADS * VD
    w_out = np.concatenate([f["w_out"][:, n_mla:], f["w_out"][:, :n_mla]], 1)
    w_out = tiles(w_out, KD, KD).reshape(L, KD, P, KD * P)
    a["w_mix"] = np.concatenate([w_in, uq, ukv, w_out], 1).reshape(L * MIX_C, P, KD * P)

    state = f["state_ret"][:, 0].reshape(L, 2, 4, 2, 32, VD)
    a["state"] = state.transpose(0, 2, 4, 3, 1, 5).reshape(L, P, 4, VD)
    cache, pe = f["cache_kv_latent"][:, 0], f["cache_k_rope"][:, 0]
    a["cache_kv"] = cache.transpose(0, 2, 1)
    a["cache_pe"] = np.tile(pe.transpose(0, 2, 1), (1, 4, 1))
    a["cache_tok"] = cache.reshape(L, 4, P, KV_RANK).transpose(0, 2, 1, 3)

    nc = _bacc.Bacc("TRN2", target_bir_lowering=False, num_devices=1)
    arrays = {f"in_{n}": np.ascontiguousarray(v) for n, v in a.items()}
    ins = {n: nc.dram_tensor(f"in_{n}", arrays[f"in_{n}"].shape, F32, kind="ExternalInput").ap() for n in a}
    outs = {n: nc.dram_tensor(f"out_{n}", shape, F32, kind="ExternalOutput").ap() for n, shape in OUTS.items()}
    streaming_trunk(nc, ins, outs)
    r = _run(nc, [arrays], core_ids=[0]).results[0]
    y, kv, kpe, st_p, st_s = (np.asarray(r[f"out_{n}"]) for n in ("y", "kv", "kpe", "state_p", "state_s"))
    y = y.transpose(1, 0, 2).reshape(D, T).T
    kv, kpe = kv.transpose(0, 2, 1)[:, None], kpe.transpose(0, 2, 1)[:, None]

    def state_of(s):
        s = s.reshape(L, 4, 32, 2, 2, VD).transpose(0, 4, 1, 3, 2, 5)
        return np.ascontiguousarray(s.reshape(L, 1, HEADS, RDK, VD))

    out = (y[None, :NP_], y[None, NP_:], kv[:, :, :NP_], kpe[:, :, :NP_], state_of(st_p),
           kv[:, :, NP_:], kpe[:, :, NP_:], state_of(st_s))
    return tuple(np.ascontiguousarray(t) for t in out)
```

```python
from contextlib import ExitStack

import numpy as np

import concourse.bass as bass
from concourse import mybir

F32 = mybir.dt.float32
F32R = mybir.dt.float32r
BF16 = mybir.dt.bfloat16
ALU = mybir.AluOpType
ACT = mybir.ActivationFunctionType
AX = mybir.AxisListType

P = 128
D = 1024
DEPTH = 2
NP_, NS = 512, 32
T = NP_ + NS
HT = T // 2
TW = T + 4
HW = TW // 2
PAST = 512
D_FF = 2816
KD = D // P
FT = D_FF // P
HEADS = 8
NOPE, ROPE, VD = 64, 32, 64
Q_RANK, KV_RANK = 256, 128
RDK = 64
EPS = 1e-6
MLA_SCALE = float((NOPE + ROPE) ** -0.5)
RET_SCALE = float(RDK ** -0.5)
NEG = -1e30

DN_T = FT // 2
UP_C = 2 * FT
DN_C = 2 * KD
Z_EARLY = 5
Z_C = Z_EARLY + 16
UQ_C = 2
MIX_C = Z_C + UQ_C + 1 + KD
OUT_C0 = Z_C + UQ_C + 1
CH = UP_C + DN_C + MIX_C + UP_C + DN_C
FFN_C = (0, UP_C + DN_C + MIX_C)
MIX_C0 = UP_C + DN_C
assert CH % 2 == 0 and UP_C % 4 == 0 and DN_C % 4 == 0 and MIX_C % 4 == 0

MODS = 9 * KD
ADA_RING = 4
ADA_A = 48
ADA_B = 24


COL_A = 2 * ADA_A // ADA_RING + 8
COL_B = 2 * ADA_B // ADA_RING + 4
N_CONST = 11

TRI = 10 * P
TRI_AT = [P * j * (j + 1) // 2 for j in range(4)]


class Signal:

    def __init__(self, sem, per_layer, before=0):
        self.sem, self.per_layer, self.before = sem, per_layer, before

    def at(self, layer, n):
        return layer * self.per_layer + (self.before + n)


def streaming_trunk(nc, a, o):
    ctx = ExitStack()
    with ctx:
        def sb(name, shape, dt=F32):
            return ctx.enter_context(nc.sbuf_tensor(name, shape, dt))

        def overlay(alternatives):
            made, size = {}, 0
            for group in alternatives:
                with ExitStack() as scope:
                    total = 0
                    for item in group:
                        if isinstance(item, list):
                            inner, more = overlay(item)
                            made.update(inner)
                            total += more
                        else:
                            name, shape, dt = item
                            made[name] = scope.enter_context(nc.sbuf_tensor(name, shape, dt))
                            total += int(np.prod(shape[1:])) * 4
                    size = max(size, total)
            return made, size

        def signal(name, per_layer, before=0):
            return Signal(ctx.enter_context(nc.semaphore(name)), per_layer, before)

        x = sb("x", [P, KD, T])
        c_all = sb("c_all", [P, 2, D])
        raw = sb("raw", [P, 2, DN_T * P])
        w_hi = sb("w_hi", [P, 2, DN_T * P], F32R)
        w_lo = sb("w_lo", [P, 2, DN_T * P], F32R)
        wide_s = sb("wide_s", [P, 2, TW])
        wide_v = sb("wide_v", [P, 2, TW])
        tmp_s, tmp_v = wide_s[:, :, 0:T], wide_v[:, :, 0:T]
        root = sb("root", [P, T])
        wide_rinv = sb("wide_rinv", [P, TW])
        rinv = wide_rinv[:, 0:T]
        squares = sb("squares", [P, T])
        ones = sb("ones", [P, P])
        mods = sb("mods", [P, 2, MODS])
        mul_pre = sb("mul_pre", [P, 3, 2, KD])
        mul_post = sb("mul_post", [P, 3, 2, KD])
        row_max, neg_max, exp_sum, inv_sum = (sb(n, [P, 8]) for n in ("row_max", "neg_max", "exp_sum", "inv_sum"))
        acc = sb("acc", [P, 2, ADA_RING])
        gains = sb("gains", [P, 3])
        junk = [tmp_v[:, v, :].bitcast(BF16)[:, 0:D] for v in range(2)]

        ident = sb("ident", [P, P])
        own_keys = [tmp_s[:, 0, :], tmp_s[:, 1, :], tmp_v[:, 0, :], tmp_v[:, 1, :]]
        half_ones = sb("half_ones", [P, P])
        k_decay = sb("k_decay", [P, 4, 4, 2])
        k_decays = sb("k_decays", [NS, HEADS])
        cross = sb("cross", [P, 4, 2, NS])
        own_head = sb("own_head", [P, 4, NS])
        state_decay = sb("state_decay", [P, 4])
        ada_b = sb("ada_b", [P, DEPTH * MODS + 16])
        g_pre = sb("g_pre", [P, DEPTH * 3 * KD + KD])
        g_post = sb("g_post", [P, DEPTH * 3 * KD])
        g_lat = sb("g_lat", [P, DEPTH * 3])
        eps = sb("eps", [P, 1])
        neg_row = sb("neg_row", [P, 64])
        scratch = sb("scratch", [P, 24])

        hm, size = overlay([
            [("h_hi", [P, KD, TW], F32R), ("h_lo", [P, KD, TW], F32R)],
            [("ada_w", [P, ADA_RING, D], F32), ("ada_end", [P, KD * TW - ADA_RING * D], F32),
             ("o_ffn", [P, KD, T], F32)],
            [("decay", [P, HEADS, 512], F32), ("q_cross", [P, 4, 2, NS], F32), ("ret_ss", [NS, HEADS, NS], F32),
             ("k_toks", [NS, 4, P], F32), ("k_tok", [P, 4, P], F32), ("ret_st", [P, 4, 512], F32)],
            [("ret_root", [P, 4, T], F32)],
            [("mla_hi", [P, 4, T], F32R), ("mla_lo", [P, 4, T], F32R),
             ("ret_hi", [P, 4, T], F32R), ("ret_lo", [P, 4, T], F32R)],
        ])
        sb("h_space", [P, size // 4])
        h_hi, h_lo, o_ffn, ada_w = hm["h_hi"], hm["h_lo"], hm["o_ffn"], hm["ada_w"]
        decay, mla_hi, mla_lo, ret_hi, ret_lo = hm["decay"], hm["mla_hi"], hm["mla_lo"], hm["ret_hi"], hm["ret_lo"]

        um, size = overlay([
            [("u_hi", [P, FT, T], F32R), ("u_lo", [P, FT, T], F32R)],
            [("kv", [P, T], F32), ("kpe", [P, T], F32), ("q_nope", [P, 4, T], F32), ("q_pe", [P, 2, T], F32),
             ("ret_v", [P, 4, T], F32), ("ret_g", [P, 4, T], F32), ("kv_tok", [P, 5, P], F32),
             ("w_ukv", [P, 8, P], F32), ("state_in", [P, 4, VD], F32), ("state_p", [P, 4, VD], F32),
             [[("ret_q", [P, 4, T], F32), ("ret_k", [P, 4, T], F32), ("kpe_swap", [P, T], F32),
               ("q_pe_swap", [P, 2, T], F32), ("rope_tab", [P, 4, T], F32),
               [[("zq", [P, 2, T], F32), ("qn_hi", [P, 2, T], F32R), ("qn_lo", [P, 2, T], F32R)],
                [("v_tok", [P, 5, 512], F32)]]],
              [("q_abs", [P, HEADS, 512], F32), ("q_abss", [P, HEADS, NS], F32), ("q_pes", [P, 2, 4, NS], F32), ("pt", [P, 2, TRI], F32),
               ("prob", [P, 2, TRI], F32),
               ("o_lat", [P, 2, 512], F32), ("o_lats", [P, HEADS, NS], F32), ("cache_kv", [P, T], F32),
               ("cache_pe", [P, T], F32), ("cache_tok", [P, 4, P], F32)]]],
            [("o_mix", [P, KD, T], F32)],
        ])
        sb("u_space", [P, size // 4])
        u_hi, u_lo, kv, kpe, q_nope, q_pe = (um[n] for n in ("u_hi", "u_lo", "kv", "kpe", "q_nope", "q_pe"))
        ret_v, ret_g, kv_tok, w_ukv, ret_q, ret_k = (
            um[n] for n in ("ret_v", "ret_g", "kv_tok", "w_ukv", "ret_q", "ret_k"))
        kpe_swap, q_pe_swap, rope_tab, v_tok, state_in, zq = (
            um[n] for n in ("kpe_swap", "q_pe_swap", "rope_tab", "v_tok", "state_in", "zq"))
        qn_hi, qn_lo, state_p, k_tok, ret_st = um["qn_hi"], um["qn_lo"], um["state_p"], hm["k_tok"], hm["ret_st"]
        ret_root, q_cross, ret_ss, k_toks = hm["ret_root"], hm["q_cross"], hm["ret_ss"], hm["k_toks"]
        q_abs, q_abss, q_pes, pt, prob, o_lat = (um[n] for n in ("q_abs", "q_abss", "q_pes", "pt", "prob", "o_lat"))
        o_lats, cache_kv, cache_pe, cache_tok, o_mix = (
            um[n] for n in ("o_lats", "cache_kv", "cache_pe", "cache_tok", "o_mix"))

        ps = ctx.enter_context(nc.psum_tensor("ps", [P, 8, 512], F32))

        def pair(b):
            return ps[:, b:b + 2, 0:HT]

        def wide_pair(b):
            return ps[:, b:b + 2, 0:HW]

        def halves(t):
            return t.rearrange("p (t n) -> p t n", t=2)

        landed = [signal(f"landed{i}", 16 * CH // 2) for i in range(2)]
        hi_done = signal("hi_done", CH)
        lo_done = signal("lo_done", CH, 2)
        w_used = signal("w_used", CH, 2)
        ada_landed = [signal(f"ada_landed{i}", 16 * MODS // ADA_RING, 16 * 16 // ADA_RING) for i in range(ADA_RING)]
        ada_done = signal("ada_done", 2 * MODS, 2 * 16)
        columns = signal("columns", COL_A + COL_B, 10)
        x_prod = signal("x_prod", 48)
        x_new = [signal(f"x_new{i}", 12, 4) for i in range(2)]
        x_sq = signal("x_sq", 24)
        sums = signal("sums", 3 * KD + 3, 2)
        sq_added = signal("sq_added", 3 * (KD - 1), 2)
        rooted = signal("rooted", 6)
        inverted = signal("inverted", 6)
        h_scaled = signal("h_scaled", 16)
        h_high = signal("h_high", 52)
        h_ready = signal("h_ready", 52)
        H_AT = (0, 18, 34)
        up_out = signal("up_out", 4 * FT, 4)
        up_silu = signal("up_silu", 4 * FT)
        up_mul = signal("up_mul", 4 * FT, 4)
        up_hi = signal("up_hi", 2 * FT)
        up_lo = signal("up_lo", 2 * FT, 2)
        out_ev = signal("out_ev", 24)
        out_sq = signal("out_sq", 24)
        z_ev = signal("z_ev", Z_C)
        m_sq = signal("m_sq", 7)
        m_sum = signal("m_sum", 7)
        m_root = signal("m_root", 6)
        m_inv = signal("m_inv", 6)
        q_scaled = signal("q_scaled", 2)
        q_high = signal("q_high", 2)
        q_low = signal("q_low", 2)
        kv_ready = signal("kv_ready", 1)
        tables = signal("tables", 16 * 2)
        decay_in = signal("decay_in", 16)
        caches = signal("caches", 16 * 3)
        rope = signal("rope", 57)
        uq_mm = signal("uq_mm", 6)
        gains_in = signal("gains_in", 1)
        uq_ev = signal("uq_ev", 8)
        ukv_in = signal("ukv_in", 1)
        tok_mm = signal("tok_mm", 7)
        tok_ev = signal("tok_ev", 7)
        kt_mm = signal("kt_mm", 5)
        kt_ev = signal("kt_ev", 5)
        rs_mm = signal("rs_mm", 4 * HEADS)
        rs_mul = signal("rs_mul", 4 * HEADS)
        ro_mm = signal("ro_mm", HEADS)
        ro_ev = signal("ro_ev", 4)
        ss_mm = signal("ss_mm", 1)
        ss_mul = signal("ss_mul", 2)
        so_mm = signal("so_mm", 1)
        so_ev = signal("so_ev", 1)
        st_mm = signal("st_mm", 4)
        st_ev = signal("st_ev", 4 * 4)
        ret_prod = signal("ret_prod", 8)
        ret_high = signal("ret_high", 4)
        ret_low = signal("ret_low", 4)
        qa_mm = signal("qa_mm", HEADS)
        qa_ev = signal("qa_ev", HEADS)
        SU = 4 * HEADS + 2
        sc_mm = signal("sc_mm", SU)
        sc_max = signal("sc_max", 2 * SU)
        sc_exp = signal("sc_exp", SU)
        sc_norm = signal("sc_norm", 2 * SU)
        at_mm = signal("at_mm", SU)
        at_ev = signal("at_ev", SU)
        pv_mm = signal("pv_mm", HEADS + 2)
        pv_ev = signal("pv_ev", HEADS + 2)
        uv_mm = signal("uv_mm", 5)
        uv_hi = signal("uv_hi", 5)
        uv_lo = signal("uv_lo", 5)
        own_in = signal("own_in", 4)
        cache_new = signal("cache_new", 4)
        stored = signal("stored", 16 * 4)
        const_in = signal("const_in", 0)
        x_in = signal("x_in", 0)
        c_in = signal("c_in", 0)
        c_act = signal("c_act", 0)
        filled = signal("filled", 0)
        y_out = signal("y_out", 0)

        ITEMS = [("p", 0), ("p", 1), ("p", 2), ("p", 3), ("s", 0), ("p", 4), ("p", 5), ("s", 1), ("p", 6), ("p", 7)]
        FIRST_UNIT = []
        n_units = 0
        for kind, _ in ITEMS:
            FIRST_UNIT.append(n_units)
            n_units += 4 if kind == "p" else 1

        block = ctx.enter_context(nc.Block())

        @block.sync
        def _(sp):
            def load_ada(tile, slot):
                sp.dma_start(ada_w[:, slot, :], a["ada"][bass.ds(tile, 1)].rearrange("a p n -> p (a n)"))\
                    .then_inc(ada_landed[slot].sem, 16)

            def load_chunk(l, c, slot, src, width):
                sp.wait_ge(lo_done.sem, lo_done.at(l, c - 1))
                sp.dma_start(raw[:, slot, 0:width], src.rearrange("a p n -> p (a n)"))\
                    .then_inc(landed[slot].sem, 16)

            sp.dma_start(c_all[:, :, :], a["c"].partition_broadcast(P)).then_inc(c_in.sem, 16)
            for t in range(ADA_RING):
                load_ada(t, t)
            sp.dma_start(x[:, :, :], a["x"]).then_inc(x_in.sem, 16)
            consts = [(ident, "ident"), (half_ones, "half_ones"), (k_decay, "k_decay"), (k_decays, "k_decays"),
                      (cross, "cross"), (own_head, "own_head"), (state_decay, "state_decay"), (ada_b, "ada_b"), (g_pre, "g_pre"),
                      (g_post, "g_post"), (g_lat, "g_lat")]
            for t, n in consts:
                sp.dma_start(t[tuple([slice(None)] * len(t.shape))], a[n]).then_inc(const_in.sem, 16)
            for t in range(ADA_RING, 16):
                sp.wait_ge(ada_done.sem, 2 * (t - ADA_RING + 1))
                load_ada(t, t % ADA_RING)

            def ffn(l, s):
                base = FFN_C[s]
                with sp.Fori(0, UP_C // 2) as i:
                    for k in range(2):
                        load_chunk(l, base + i * 2 + k, k, a["w_up"][bass.ds((l * 2 + s) * UP_C + i * 2 + k, 1)], KD * P)
                first, per = ((0, ADA_A // 4), (ADA_A, ADA_B // 3))[s]

                def down(i, first_time=False, ada=True):
                    for k in range(4):
                        load_chunk(l, base + UP_C + i * 4 + k, k % 2,
                                   a["w_dn"][bass.ds((l * 2 + s) * DN_C + i * 4 + k, 1)], DN_T * P)
                        if first_time:
                            tiles = (0, 0, ADA_RING, (per + ADA_RING) // 2, per)[k:k + 2]
                        else:
                            tiles = (k * per // 4, (k + 1) * per // 4)
                        for t in range(*tiles) if ada else ():
                            if not first_time or t >= ADA_RING:
                                sp.wait_ge(ada_done.sem, ada_done.at(l, 2 * first + 2 * per * i + 2 * (t - ADA_RING + 1)))
                            elif t == 0:
                                sp.wait_ge(w_used.sem, w_used.at(l, base + UP_C))
                            load_ada(l * MODS + 16 + first + i * per + t, t % ADA_RING)

                down(0, first_time=True)
                with sp.Fori(1, 4 - s) as i:
                    down(i)
                if s == 1:
                    down(3, ada=False)

            with sp.Fori(0, DEPTH) as l:
                ffn(l, 0)
                for c in range(MIX_C):
                    load_chunk(l, MIX_C0 + c, c % 2, a["w_mix"][bass.ds(l * MIX_C + c, 1)], KD * P)
                    if c == 1:
                        sp.wait_ge(w_used.sem, w_used.at(l, MIX_C0))
                        sp.dma_start(rope_tab[:, :, :], a["rope"]).then_inc(tables.sem, 16)
                        sp.dma_start(state_in[:, :, :], a["state"][bass.ds(l, 1)].rearrange("a p i v -> p (a i) v"))\
                            .then_inc(tables.sem, 16)
                    if c == Z_C + 1:
                        sp.wait_ge(w_used.sem, w_used.at(l, MIX_C0 + Z_C))
                        sp.dma_start(decay[:, :, :], a["decay"]).then_inc(decay_in.sem, 16)
                    if c == OUT_C0 + 1:
                        sp.wait_ge(kv_ready.sem, kv_ready.at(l, 1))
                        sp.dma_start(o["kv"][bass.ds(l, 1)].rearrange("a p n -> p (a n)"), kv[:, :]).then_inc(stored.sem, 16)
                        sp.wait_ge(rope.sem, rope.at(l, 3))
                        sp.dma_start(o["kpe"][bass.ds(l, 1)].rearrange("a p n -> p (a n)"), kpe[0:ROPE, :]).then_inc(stored.sem, 16)
                        sp.wait_ge(st_ev.sem, st_ev.at(l, 16))
                        sp.dma_start(o["state_p"][bass.ds(l, 1)].rearrange("a p i v -> p (a i) v"), state_p[:, :, :])\
                            .then_inc(stored.sem, 16)
                        sp.dma_start(o["state_s"][bass.ds(l, 1)].rearrange("a p i v -> p (a i) v"), state_in[:, :, :])\
                            .then_inc(stored.sem, 16)
                        sp.wait_ge(ro_mm.sem, ro_mm.at(l, HEADS))
                        sp.dma_start(cache_kv[:, 0:PAST], a["cache_kv"][bass.ds(l, 1)].rearrange("a p n -> p (a n)"))\
                            .then_inc(caches.sem, 16)
                        sp.dma_start(cache_pe[:, 0:PAST], a["cache_pe"][bass.ds(l, 1)].rearrange("a p n -> p (a n)"))\
                            .then_inc(caches.sem, 16)
                        sp.dma_start(cache_tok[:, :, :], a["cache_tok"][bass.ds(l, 1)].rearrange("a p b r -> p (a b) r"))\
                            .then_inc(caches.sem, 16)
                ffn(l, 1)
            for new in x_new:
                sp.wait_ge(new.sem, new.at(DEPTH, 0))
            sp.dma_start(o["y"], x[:, :, :]).then_inc(y_out.sem, 16)
            sp.wait_ge(y_out.sem, 16)
            sp.wait_ge(stored.sem, stored.at(DEPTH, 0))

        @block.gpsimd
        def _(pool):
            for k in range(2):
                pool.memset(scratch[:, k:k + 1], 0.0).then_inc(lo_done.sem, 1)
                pool.memset(scratch[:, 14 + k:15 + k], 0.0).then_inc(sq_added.sem, 1)

            def low(l, c, slot, width):
                pool.wait_ge(hi_done.sem, hi_done.at(l, c + 1))
                pool.tensor_tensor(w_lo[:, slot, 0:width], raw[:, slot, 0:width], w_hi[:, slot, 0:width].bitcast(F32),
                                   ALU.subtract).then_inc(lo_done.sem, 1)

            def add_square(l, j, m, buf):
                pool.wait_ge(out_sq.sem, out_sq.at(l, j * KD + m + 1))
                pool.wait_ge(sq_added.sem, sq_added.at(l, j * (KD - 1) + m))
                pool.tensor_tensor(squares[:, :], squares[:, :], tmp_s[:, buf, :], ALU.add).then_inc(sq_added.sem, 1)

            def add_first_squares(l, j):
                pool.wait_ge(out_sq.sem, out_sq.at(l, j * KD + 2))
                pool.tensor_tensor(squares[:, :], tmp_s[:, 0, :], tmp_s[:, 1, :], ALU.add).then_inc(sq_added.sem, 2)

            def add_odd(l, j):
                for m in range(1, KD - 1, 2):
                    pool.wait_ge(x_prod.sem, x_prod.at(l, j * 16 + 2 * m + 2))
                    pool.tensor_tensor(x[:, m, :], x[:, m, :], tmp_v[:, 1, :], ALU.add).then_inc(x_new[1].sem, 1)

            def ffn(l, s):
                with pool.Fori(0, UP_C // 2) as i:
                    for k in range(2):
                        low(l, FFN_C[s] + i * 2 + k, k, KD * P)
                for i in range(3):
                    for k in range(2):
                        low(l, FFN_C[s] + UP_C + i * 2 + k, k, DN_T * P)
                add_first_squares(l, 2 * s)
                with pool.Fori(0, 2) as i:
                    for m in range(2):
                        for k in range(2):
                            low(l, FFN_C[s] + UP_C + i * 4 + 2 * (m + 3) + k, k, DN_T * P)
                        add_square(l, 2 * s, i * 2 + m + 2, m)
                for k in range(2):
                    low(l, FFN_C[s] + UP_C + 2 * (KD - 1) + k, k, DN_T * P)
                add_square(l, 2 * s, KD - 2, 0)
                add_odd(l, 2 * s)

            with pool.Fori(0, DEPTH) as l:
                ffn(l, 0)
                with pool.Fori(0, (OUT_C0 + 4) // 2) as i:
                    for k in range(2):
                        low(l, MIX_C0 + i * 2 + k, k, KD * P)
                add_first_squares(l, 1)
                for m in range(2, KD - 1):
                    if m < KD - 2:
                        low(l, MIX_C0 + OUT_C0 + m + 2, m % 2, KD * P)
                    add_square(l, 1, m, m % 2)
                add_odd(l, 1)
                ffn(l, 1)

        @block.tensor
        def _(pe):
            pe.wait_ge(filled.sem, 1)
            for n, sig in enumerate((w_used, sums)):
                for k in range(2):
                    pe.matmul(ps[:, 2 * n + k, 0:P], ones[:, :], ones[:, :], start=True, stop=True).then_inc(sig.sem, 1)

            def tile3(bank, slot, kk, hi, lo, start, stop, half=HT):
                wh = w_hi[:, slot, kk * P:(kk + 1) * P]
                wl = w_lo[:, slot, kk * P:(kk + 1) * P]
                for t in range(2):
                    n = slice(t * half, (t + 1) * half)
                    pe.matmul(ps[:, bank + t, 0:half], wh, hi[:, n], start=start, stop=False)
                    pe.matmul(ps[:, bank + t, 0:half], wh, lo[:, n], start=False, stop=False)
                for t in range(2):
                    n = slice(t * half, (t + 1) * half)
                    last = pe.matmul(ps[:, bank + t, 0:half], wl, hi[:, n], start=False, stop=stop)
                return last

            def add_squares(src, bank, start, stop, mat):
                for t in range(2):
                    last = pe.matmul(ps[:, bank + t, 0:HT], mat[:, :], src[:, t * HT:(t + 1) * HT],
                                     start=start, stop=stop)
                return last

            def pre_norm(l, j):
                for m in range(KD):
                    pe.wait_ge(x_sq.sem, x_sq.at(l, j * KD + m + 1))
                    add_squares(tmp_s[:, m % 2, :], 6, m == 0, m == KD - 1, ones).then_inc(sums.sem, 1)

            def up(l, s):
                base = FFN_C[s]
                with pe.Fori(0, FT // 2) as i:
                    for f in range(2):
                        pe.wait_ge(up_out.sem, up_out.at(l, 2 * s * FT + i * 4 + 2 * f - 2))
                        if f == 1:
                            pe.wait_ge(rooted.sem, rooted.at(l, 4 * s + 1))
                        for w in range(2):
                            pe.wait_ge(lo_done.sem, lo_done.at(l, base + i * 4 + 2 * f + w + 1))
                            for k in range(KD):
                                if f == 0 and w == 0:
                                    pe.wait_ge(h_ready.sem, h_ready.at(l, H_AT[2 * s] + 2 + 2 * k + 2))
                                last = tile3(4 * f + 2 * w, w, k, h_hi[:, k, :], h_lo[:, k, :], k == 0, k == KD - 1, HW)
                            last.then_inc(w_used.sem, 1)

            def out_tiles(l, j, chunk0, per_tile, chunk_tiles, operand, ready):
                def tile(m, mm, first):
                    if not first:
                        pe.wait_ge(out_sq.sem, out_sq.at(l, j * KD + m - 1))
                    k = 0
                    for q in range(per_tile):
                        n = m * per_tile + q
                        pe.wait_ge(lo_done.sem, lo_done.at(l, chunk0 + n + 1))
                        for kk in range(chunk_tiles):
                            if first:
                                ready(k)
                            hi, lo = operand(k)
                            last = tile3(2 * mm, (q + mm * per_tile + chunk0) % 2, kk, hi, lo,
                                         k == 0, k == per_tile * chunk_tiles - 1)
                            k += 1
                        last.then_inc(w_used.sem, 1)

                tile(0, 0, True)
                tile(1, 1, True)
                with pe.Fori(1, KD // 2) as i:
                    tile(i * 2, 0, False)
                    tile(i * 2 + 1, 1, False)
                pe.wait_ge(sq_added.sem, sq_added.at(l, (j + 1) * (KD - 1)))
                add_squares(squares[:, :], 4, True, False, ones)
                pe.wait_ge(out_sq.sem, out_sq.at(l, (j + 1) * KD))
                add_squares(tmp_s[:, 1, :], 4, False, True, ones).then_inc(sums.sem, 1)

            def ffn(l, s):
                pre_norm(l, 2 * s)
                up(l, s)

                def ready(k):
                    if k in (0, FT - 2, FT - 1):
                        pe.wait_ge(up_lo.sem, up_lo.at(l, s * FT + max(k + 1, FT - 2)))

                out_tiles(l, 2 * s, FFN_C[s] + UP_C, 2, DN_T, lambda k: (u_hi[:, k, :], u_lo[:, k, :]), ready)

            def mixer(l):
                pre_norm(l, 1)

                def z_tile(z, bank, slot, first):
                    if not first:
                        pe.wait_ge(z_ev.sem, z_ev.at(l, z - 1))
                    pe.wait_ge(lo_done.sem, lo_done.at(l, MIX_C0 + z + 1))
                    for k in range(KD):
                        if first:
                            pe.wait_ge(h_ready.sem, h_ready.at(l, H_AT[1] + 2 * k + 2))
                        last = tile3(bank, slot, k, h_hi[:, k, :], h_lo[:, k, :], k == 0, k == KD - 1)
                    last.then_inc(w_used.sem, 1)

                def norm_sum(n, buf, bank, start, stop, mat=ones):
                    pe.wait_ge(m_sq.sem, m_sq.at(l, n + 1))
                    add_squares(tmp_s[:, buf, :], bank, start, stop, mat).then_inc(m_sum.sem, 1)

                for z in range(Z_EARLY):
                    z_tile(z, 2 * (z % 2), z % 2, z < 2)
                    if z == 2:
                        norm_sum(0, 0, 4, True, False)
                        norm_sum(1, 1, 4, False, True)
                    if z == 3:
                        norm_sum(2, 0, 6, True, True)
                with pe.Fori(0, 4) as i:
                    for t in range(4):
                        z = Z_EARLY + t
                        z_tile(i * 4 + z, 2 * (z % 2), z % 2, False)

                for c in range(UQ_C):
                    pe.wait_ge(lo_done.sem, lo_done.at(l, MIX_C0 + Z_C + c + 1))
                    for oo in range(4):
                        n = 4 * c + oo
                        if n < 2:
                            pe.wait_ge(z_ev.sem, z_ev.at(l, Z_C))
                        else:
                            pe.wait_ge(uq_ev.sem, uq_ev.at(l, n - 1))
                        for k in range(2):
                            if n == 0:
                                pe.wait_ge(q_low.sem, q_low.at(l, k + 1))
                            last = tile3(2 * (n % 2), (Z_C + c) % 2, 2 * oo + k, qn_hi[:, k, :], qn_lo[:, k, :],
                                         k == 0, k == 1)
                        last.then_inc((w_used if oo == 3 else uq_mm).sem, 1)

                pe.wait_ge(ukv_in.sem, ukv_in.at(l, 1))
                pe.wait_ge(m_root.sem, m_root.at(l, 2))
                for b in range(5):
                    w = P if b < 4 else NS
                    bank = 4 + b % 4
                    if b == 4:
                        pe.wait_ge(tok_ev.sem, tok_ev.at(l, 1))
                    for i in range(4):
                        last = pe.transpose(ps[0:w, bank, i * P:(i + 1) * P], ret_v[:, i, b * P:b * P + w], ident[:, :])
                        if b == 0 and i == 0:
                            last.then_inc(w_used.sem, 1)
                    last.then_inc(tok_mm.sem, 1)
                pe.wait_ge(kv_ready.sem, kv_ready.at(l, 1))
                pe.wait_ge(tok_ev.sem, tok_ev.at(l, 2))
                for b in range(4):
                    last = pe.transpose(ps[:, 5, b * P:(b + 1) * P], kv[:, b * P:(b + 1) * P], ident[:, :])
                last.then_inc(tok_mm.sem, 1)
                pe.wait_ge(tok_ev.sem, tok_ev.at(l, 3))
                pe.transpose(ps[0:NS, 6, 0:P], kv[:, 512:T], ident[:, :]).then_inc(tok_mm.sem, 1)

                pe.wait_ge(rope.sem, rope.at(l, 51))
                pe.wait_ge(uq_ev.sem, uq_ev.at(l, 8))
                pe.wait_ge(tok_ev.sem, tok_ev.at(l, 6))
                for i in range(4):
                    last = pe.transpose(ps[0:NS, 5, i * P:(i + 1) * P], ret_k[:, i, 512:T], ident[:, :])
                last.then_inc(kt_mm.sem, 1)
                for h in range(HEADS):
                    rows = slice(64 * (h % 2), 64 * (h % 2) + 64)
                    last = pe.matmul(ps[0:NS, h % 2, (h // 2) * NS:(h // 2 + 1) * NS], ret_k[rows, h // 2, 512:T],
                                     ret_q[rows, h // 2, 512:T], start=True, stop=True)
                last.then_inc(ss_mm.sem, 1)
                pe.wait_ge(tok_ev.sem, tok_ev.at(l, 7))
                pe.wait_ge(ss_mul.sem, ss_mul.at(l, 2))
                pe.wait_ge(tables.sem, tables.at(l, 32))
                for h in range(HEADS):
                    rows = slice(64 * (h % 2), 64 * (h % 2) + 64)
                    dst = ps[rows, 7, (h // 2) * NS:(h // 2 + 1) * NS]
                    pe.matmul(dst, v_tok[0:NS, 4, h * VD:(h + 1) * VD], ret_ss[:, h, :], start=True, stop=False)
                    last = pe.matmul(dst, state_in[:, h // 2, :], q_cross[:, h // 2, h % 2, :], start=False, stop=True)
                last.then_inc(so_mm.sem, 1)

                def ret_scores(h):
                    rows = slice(64 * (h % 2), 64 * (h % 2) + 64)
                    for b in range(4):
                        if h:
                            pe.wait_ge(rs_mul.sem, rs_mul.at(l, 4 * (h - 1) + b + 1))
                        pe.matmul(ps[:, b, 0:512 - b * P], ret_k[rows, h // 2, b * P:(b + 1) * P],
                                  ret_q[rows, h // 2, b * P:512], start=True, stop=True).then_inc(rs_mm.sem, 1)

                def state(i):
                    pe.wait_ge(kt_ev.sem, kt_ev.at(l, 1 + i))
                    for b in range(4):
                        last = pe.transpose(ps[:, 4, b * P:(b + 1) * P], ret_k[:, i, b * P:(b + 1) * P], ident[:, :])
                    last.then_inc(kt_mm.sem, 1)

                def state_mm(i):
                    pe.wait_ge(kt_ev.sem, kt_ev.at(l, 2 + i))
                    if i:
                        pe.wait_ge(st_ev.sem, st_ev.at(l, 4 * i))
                    for b in range(4):
                        pe.matmul(ps[:, 5, 0:P], k_tok[:, b, :], v_tok[:, b, i * P:(i + 1) * P],
                                  start=b == 0, stop=b == 3)
                    pe.matmul(ps[:, 5, P:2 * P], k_toks[:, i, :], v_tok[0:NS, 4, i * P:(i + 1) * P],
                              start=True, stop=True).then_inc(st_mm.sem, 1)

                ret_scores(0)
                for h in range(HEADS):
                    if h < HEADS - 1:
                        ret_scores(h + 1)
                    if h % 2 == 0:
                        state(h // 2)
                    else:
                        state_mm(h // 2)
                    rows = slice(64 * (h % 2), 64 * (h % 2) + 64)
                    bank = 6 + (h // 2) % 2
                    if h == 2:
                        pe.wait_ge(so_ev.sem, so_ev.at(l, 1))
                    if h >= 4:
                        pe.wait_ge(ro_ev.sem, ro_ev.at(l, h // 2 - 1))
                    for b in range(4):
                        pe.wait_ge(rs_mul.sem, rs_mul.at(l, 4 * h + b + 1))
                        last = pe.matmul(ps[rows, bank, b * P:512], v_tok[:, b, h * VD:(h + 1) * VD],
                                         ret_st[:, b, 0:512 - b * P], start=b == 0, stop=b == 3)
                    last.then_inc(ro_mm.sem, 1)

                pe.wait_ge(st_ev.sem, st_ev.at(l, 16))
                for h in range(HEADS):
                    rows = slice(64 * (h % 2), 64 * (h % 2) + 64)
                    if h >= 2:
                        pe.wait_ge(qa_ev.sem, qa_ev.at(l, h - 1))
                    else:
                        pe.wait_ge(rs_mul.sem, rs_mul.at(l, 32))
                    for t, n in enumerate((slice(0, 512), slice(512, T))):
                        last = pe.matmul(ps[:, 2 * (h % 2) + t, 0:n.stop - n.start], w_ukv[rows, h // 2, :],
                                         q_nope[rows, h // 2, n], start=True, stop=True)
                    last.then_inc(qa_mm.sem, 1)
                    if h % 2:
                        n = h // 2
                        if n >= 2:
                            pe.wait_ge(m_root.sem, m_root.at(l, 2 + n - 1))
                        elif n == 0:
                            pe.wait_ge(st_ev.sem, st_ev.at(l, 16))
                        else:
                            pe.wait_ge(ro_ev.sem, ro_ev.at(l, 4))
                        norm_sum(3 + n, n % 2, 4 + 2 * (n % 2), True, True, half_ones)

                bank_exp = {0: 0, 1: 0, 2: 0, 3: 0}
                def scores(n):
                    kind, h = ITEMS[n]
                    u = FIRST_UNIT[n]
                    if n == 0:
                        pe.wait_ge(own_in.sem, own_in.at(l, 4))
                    if kind == "p":
                        for j in range(4):
                            if n == 0:
                                pe.wait_ge(qa_ev.sem, qa_ev.at(l, HEADS))
                            if bank_exp[j]:
                                pe.wait_ge(sc_exp.sem, sc_exp.at(l, bank_exp[j]))
                            q = slice(j * P, (j + 1) * P)
                            w = (j + 1) * P
                            pe.matmul(ps[:, j, 0:w], q_abs[:, h, q], kv[:, 0:w], start=True, stop=False)
                            pe.matmul(ps[0:64, j, w - 64:w], ones[:, 0:64], neg_row[:, :], start=False, stop=False,
                                      skip_group_check=True)
                            pe.matmul(ps[:, j, 0:w], q_pe[:, h // 4, q], own_keys[h % 4][:, 0:w], start=False, stop=True)\
                                .then_inc(sc_mm.sem, 1)
                            bank_exp[j] = u + j + 1
                        return
                    pe.wait_ge(caches.sem, caches.at(l, 48))
                    pe.wait_ge(cache_new.sem, cache_new.at(l, 4))
                    for t in range(2):
                        pe.wait_ge(sc_exp.sem, sc_exp.at(l, bank_exp[t]))
                        k = slice(t * HT, (t + 1) * HT)
                        pe.matmul(ps[:, t, 0:HT], q_abss[:, 4 * h:4 * h + 4, :].rearrange("p h n -> p (h n)"),
                                  cache_kv[:, k], start=True, stop=False)
                        last = pe.matmul(ps[:, t, 0:HT], q_pes[:, h, :, :].rearrange("p h n -> p (h n)"), cache_pe[:, k],
                                         start=False, stop=True)
                        bank_exp[t] = u + 1
                    last.then_inc(sc_mm.sem, 1)

                def turned(n):
                    kind, h = ITEMS[n]
                    if n == 0:
                        pe.wait_ge(m_root.sem, m_root.at(l, 6))
                    for j in range(4 if kind == "p" else 1):
                        u = FIRST_UNIT[n] + j
                        if u >= 2:
                            pe.wait_ge(at_ev.sem, at_ev.at(l, u - 1))
                        pe.wait_ge(sc_norm.sem, sc_norm.at(l, 2 * u + 2))
                        blocks = j + 1 if kind == "p" else 4
                        for kb in range(blocks):
                            last = pe.transpose(ps[:, 4 + u % 2, kb * P:(kb + 1) * P],
                                                prob[:, n % 2, TRI_AT[j] + kb * P:TRI_AT[j] + (kb + 1) * P], ident[:, :])
                        if kind == "s":
                            pe.wait_ge(pv_ev.sem, pv_ev.at(l, n))
                            last = pe.transpose(ps[0:NS, 6, 0:P], prob[:, n % 2, 512:T], ident[:, :])
                        last.then_inc(at_mm.sem, 1)

                def values(n):
                    kind, h = ITEMS[n]
                    if n:
                        pe.wait_ge(pv_ev.sem, pv_ev.at(l, n))
                    units = FIRST_UNIT[n] + (4 if kind == "p" else 1)
                    pe.wait_ge(at_ev.sem, at_ev.at(l, units))
                    if kind == "p":
                        for j in range(4):
                            for kb in range(j + 1):
                                at = TRI_AT[j] + kb * P
                                last = pe.matmul(ps[:, 6, j * P:(j + 1) * P], kv_tok[:, kb, :], pt[:, n % 2, at:at + P],
                                                 start=kb == 0, stop=kb == j)
                    else:
                        for kb in range(4):
                            pe.matmul(ps[:, 6, 0:P], cache_tok[:, kb, :], pt[:, n % 2, kb * P:(kb + 1) * P],
                                      start=kb == 0, stop=False)
                        last = pe.matmul(ps[:, 6, 0:P], kv_tok[0:NS, 4, :], pt[0:NS, n % 2, 512:512 + P],
                                         start=False, stop=True)
                    last.then_inc(pv_mm.sem, 1)

                def heads_out(n):
                    kind, h = ITEMS[n]
                    if kind == "s":
                        return
                    pe.wait_ge(pv_ev.sem, pv_ev.at(l, n + 1))
                    rows = slice(64 * (h % 2), 64 * (h % 2) + 64)
                    if h % 2 == 0 and h:
                        pe.wait_ge(uv_lo.sem, uv_lo.at(l, h // 2))
                    last = pe.matmul(ps[rows, 7, :], w_ukv[:, 4 + h // 2, rows], o_lat[:, h % 2, :], start=True, stop=True)
                    if h % 2:
                        last.then_inc(uv_mm.sem, 1)

                scores(0)
                for n in range(len(ITEMS)):
                    if n + 1 < len(ITEMS):
                        scores(n + 1)
                    turned(n)
                    if n:
                        heads_out(n - 1)
                    values(n)
                heads_out(len(ITEMS) - 1)
                for h in range(HEADS):
                    rows = slice(64 * (h % 2), 64 * (h % 2) + 64)
                    last = pe.matmul(ps[rows, 6, (h // 2) * NS:(h // 2 + 1) * NS], w_ukv[:, 4 + h // 2, rows],
                                     o_lats[:, h, :], start=True, stop=True)
                last.then_inc(uv_mm.sem, 1)

                def ready(k):
                    if k == 0:
                        pe.wait_ge(ret_low.sem, ret_low.at(l, 4))
                        pe.wait_ge(at_ev.sem, at_ev.at(l, SU))
                    if k >= 4:
                        pe.wait_ge(uv_lo.sem, uv_lo.at(l, 5))

                def operand(k):
                    return (ret_hi[:, k, :], ret_lo[:, k, :]) if k < 4 else (mla_hi[:, k - 4, :], mla_lo[:, k - 4, :])

                out_tiles(l, 1, MIX_C0 + OUT_C0, 1, KD, operand, ready)

            with pe.Fori(0, DEPTH) as l:
                ffn(l, 0)
                mixer(l)
                ffn(l, 1)

        @block.scalar
        def _(act):
            def used(l, c):
                act.wait_ge(w_used.sem, w_used.at(l, c + 1))

            def high(l, c, slot, width):
                act.wait_ge(w_used.sem, w_used.at(l, c - 1))
                act.wait_ge(landed[slot].sem, landed[slot].at(l, 16 * (c // 2) + 16))
                nc.scalar.copy(w_hi[:, slot, 0:width], raw[:, slot, 0:width]).then_inc(hi_done.sem, 1)

            def high_at(l, base, i2, k, width):
                c = base + 2 * i2 + k
                act.wait_ge(w_used.sem, w_used.at(l, c - 1))
                act.wait_ge(landed[k].sem, landed[k].at(l, 16 * (base // 2) + 16 * i2 + 16))
                nc.scalar.copy(w_hi[:, k, 0:width], raw[:, k, 0:width]).then_inc(hi_done.sem, 1)

            def root_of(l, sig, n, bank, count):
                nc.scalar.activation(halves(root[:, :]), pair(bank), ACT.Sqrt, bias=eps[:, 0:1],
                                     scale=1.0 / count).then_inc(sig.sem, 1)

            def pre_norm(l, j, next_chunk):
                for k in range(2):
                    high(l, next_chunk + k, k, KD * P)
                for m in range(KD):
                    act.wait_ge(x_new[m % 2].sem, x_new[m % 2].at(l, (j - 1) * (KD // 2) + m // 2 + 1))
                    act.wait_ge(sums.sem, sums.at(l, j * (KD + 1) + m - 1))
                    nc.scalar.activation(tmp_s[:, m % 2, :], x[:, m, :], ACT.Square).then_inc(x_sq.sem, 1)
                act.wait_ge(sums.sem, sums.at(l, j * (KD + 1) + KD))
                root_of(l, rooted, 2 * j, 6, D)
                act.wait_ge(columns.sem, columns.at(l, COL_A))
                for m in range(KD):
                    act.wait_ge(h_scaled.sem, h_scaled.at(l, 2 * m + 2))
                    for v, n in enumerate((slice(0, NP_), slice(NP_, T))):
                        c = 3 * j * KD + m
                        nc.scalar.activation(h_hi[:, m, n], tmp_v[:, m % 2, n], ACT.Identity,
                                             bias=mods[:, v, c:c + 1]).then_inc(h_high.sem, 1)

            def pre_scale(l, j, next_chunk):
                act.wait_ge(columns.sem, columns.at(l, COL_A if j else 0))
                for v in range(2):
                    c = 3 * j * KD
                    nc.scalar.copy(h_hi[:, :, T + 2 * v:T + 2 * v + 2],
                                   mods[:, v, c:c + KD].unsqueeze(2).to_broadcast([P, KD, 2])).then_inc(h_high.sem, 1)
                for k in range(2):
                    high(l, next_chunk + k, k, KD * P)
                for m in range(KD):
                    act.wait_ge(x_new[m % 2].sem, x_new[m % 2].at(l, (j - 1) * (KD // 2) + m // 2 + 1))
                    act.wait_ge(sums.sem, sums.at(l, j * (KD + 1) + m - 1))
                    nc.scalar.activation(tmp_s[:, m % 2, :], x[:, m, :], ACT.Square).then_inc(x_sq.sem, 1)
                    for v, n in enumerate((slice(0, NP_), slice(NP_, T))):
                        nc.scalar.activation(h_hi[:, m, n], x[:, m, n], ACT.Copy,
                                             scale=mul_pre[:, j, v, m:m + 1]).then_inc(h_high.sem, 1)
                act.wait_ge(sums.sem, sums.at(l, j * (KD + 1) + KD))
                root_of(l, rooted, 2 * j, 6, D)

            def up(l, s):
                base = FFN_C[s]

                def tile(i, f, last_width):
                    n = s * FT + i * 2 + f
                    for k in range(2):
                        high_at(l, base, i * 2 + f + 1, k, last_width if f else KD * P)
                    act.wait_ge(up_out.sem, up_out.at(l, 2 * n + 1))
                    for v, at in enumerate((slice(0, NP_), slice(NP_, T))):
                        nc.scalar.activation(wide_s[:, f, at], wide_s[:, f, at], ACT.Silu,
                                             bias=wide_s[:, f, T + 2 * v:T + 2 * v + 1]).then_inc(up_silu.sem, 1)
                    act.wait_ge(up_mul.sem, up_mul.at(l, 2 * n + 2))
                    nc.scalar.copy(u_hi[:, bass.ds(i * 2 + f, 1), :].rearrange("p a n -> p (a n)"),
                                   tmp_v[:, f, :]).then_inc(up_hi.sem, 1)

                with act.Fori(0, FT // 2 - 1) as i:
                    tile(i, 0, KD * P)
                    tile(i, 1, KD * P)
                tile(FT // 2 - 1, 0, KD * P)
                tile(FT // 2 - 1, 1, DN_T * P)

            def out_tiles(l, j, chunk0, per_tile, chunk_tiles, o_buf):
                def tile(m, mm, i2):
                    if i2 is not None and per_tile == 2:
                        for k in range(2):
                            high_at(l, chunk0, m + 1, k, chunk_tiles * P)
                    elif i2 is not None:
                        high_at(l, chunk0, i2, mm, chunk_tiles * P)
                    act.wait_ge(w_used.sem, w_used.at(l, chunk0 + (m + 1) * per_tile))
                    o_tile = o_buf[:, bass.ds(m, 1), :].rearrange("p a (t n) -> p (a t) n", t=2)
                    nc.scalar.copy(o_tile, pair(2 * mm)).then_inc(out_ev.sem, 1)
                    act.wait_ge(sq_added.sem, sq_added.at(l, j * (KD - 1) + m - 1))
                    nc.scalar.activation(halves(tmp_s[:, mm, :]), pair(2 * mm), ACT.Square).then_inc(out_sq.sem, 1)

                with act.Fori(0, KD // 2 - 1) as i:
                    for mm in range(2):
                        tile(i * 2 + mm, mm, i + 1)
                tile(KD - 2, 0, KD // 2 if per_tile == 2 else None)
                tile(KD - 1, 1, None)
                act.wait_ge(sums.sem, sums.at(l, (j + 1) * (KD + 1)))
                root_of(l, rooted, 2 * j + 1, 4, D)

            def ffn(l, s):
                pre_scale(l, 2 * s, FFN_C[s])
                up(l, s)
                out_tiles(l, 2 * s, FFN_C[s] + UP_C, 2, DN_T, o_ffn)

            def mixer(l):
                pre_norm(l, 1, MIX_C0)

                def z_out(z, bank, dst, func=ACT.Copy):
                    act.wait_ge(w_used.sem, w_used.at(l, MIX_C0 + z + 1))
                    nc.scalar.activation(dst, pair(bank), func).then_inc(z_ev.sem, 1)

                def square(n, buf, src):
                    nc.scalar.activation(tmp_s[:, buf, :], src, ACT.Square).then_inc(m_sq.sem, 1)

                early = [zq[:, 0, :], zq[:, 1, :], kv[:, :], kpe[:, :], kpe_swap[:, :]]
                for z in range(Z_EARLY):
                    high(l, MIX_C0 + z + 2, z % 2, KD * P)
                    z_out(z, 2 * (z % 2), halves(early[z]))
                    if z < 3:
                        act.wait_ge(z_ev.sem, z_ev.at(l, z + 1))
                        if z == 2:
                            act.wait_ge(m_sum.sem, m_sum.at(l, 1))
                        square(z, z % 2, early[z])
                    if z == 3:
                        act.wait_ge(m_sum.sem, m_sum.at(l, 2))
                        root_of(l, m_root, 0, 4, Q_RANK)
                    if z == 4:
                        act.wait_ge(m_sum.sem, m_sum.at(l, 3))
                        act.wait_ge(m_inv.sem, m_inv.at(l, 1))
                        root_of(l, m_root, 1, 6, KV_RANK)
                        for k in range(2):
                            act.wait_ge(q_scaled.sem, q_scaled.at(l, k + 1))
                            nc.scalar.copy(qn_hi[:, k, :], tmp_v[:, k, :]).then_inc(q_high.sem, 1)
                for first, tensors in ((Z_EARLY, (ret_q, ret_k)), (Z_EARLY + 8, (ret_v, ret_g))):
                    with act.Fori(0, 2) as i:
                        for t in range(4):
                            z = first + t
                            c = MIX_C0 + z + 2
                            dst = tensors[t // 2]
                            act.wait_ge(w_used.sem, w_used.at(l, i * 4 + c - 1))
                            act.wait_ge(landed[z % 2].sem, landed[z % 2].at(l, i * 32 + 16 * (c // 2) + 16))
                            nc.scalar.copy(w_hi[:, z % 2, 0:KD * P], raw[:, z % 2, 0:KD * P]).then_inc(hi_done.sem, 1)
                            z_out(i * 4 + z, 2 * (z % 2),
                                  dst[:, bass.ds(2 * i + t % 2, 1), :].rearrange("p a (t n) -> p (a t) n", t=2),
                                  ACT.Silu if dst is ret_g else ACT.Copy)
                uq_dst = [q_nope[:, n, :] for n in range(4)] + [q_pe[:, n, :] for n in range(2)] + \
                         [q_pe_swap[:, n, :] for n in range(2)]
                for n in range(8):
                    if n == 4:
                        act.wait_ge(landed[(Z_C + UQ_C) % 2].sem, landed[(Z_C + UQ_C) % 2].at(l, 16 * ((MIX_C0 + Z_C + UQ_C) // 2) + 16))
                        nc.scalar.copy(w_ukv[:, :, :].rearrange("p a n -> p (a n)"),
                                       raw[:, (Z_C + UQ_C) % 2, 0:KD * P]).then_inc(ukv_in.sem, 1)
                        high(l, MIX_C0 + Z_C + UQ_C, (Z_C + UQ_C) % 2, KD * P)
                    if n % 4 == 3:
                        used(l, MIX_C0 + Z_C + n // 4)
                    else:
                        act.wait_ge(uq_mm.sem, uq_mm.at(l, n - n // 4 + 1))
                    nc.scalar.copy(halves(uq_dst[n]), pair(2 * (n % 2))).then_inc(uq_ev.sem, 1)
                high(l, MIX_C0 + OUT_C0, OUT_C0 % 2, KD * P)
                for n in range(7):
                    act.wait_ge(tok_mm.sem, tok_mm.at(l, n + 1))
                    if n < 5:
                        w = P if n < 4 else NS
                        nc.scalar.copy(v_tok[0:w, n, :], ps[0:w, 4 + n % 4, :])\
                            .then_inc(tok_ev.sem, 1)
                    elif n == 5:
                        nc.scalar.copy(kv_tok[:, 0:4, :].rearrange("p a n -> p (a n)"), ps[:, 5, :]).then_inc(tok_ev.sem, 1)
                    else:
                        nc.scalar.copy(kv_tok[0:NS, 4, :], ps[0:NS, 6, 0:P]).then_inc(tok_ev.sem, 1)
                high(l, MIX_C0 + OUT_C0 + 1, 1, KD * P)
                act.wait_ge(so_mm.sem, so_mm.at(l, 1))
                nc.scalar.copy(ret_v[:, :, 512:T], ps[:, 7, 0:4 * NS].rearrange("p (a n) -> p a n", a=4))\
                    .then_inc(so_ev.sem, 1)
                for n in range(4):
                    act.wait_ge(ro_mm.sem, ro_mm.at(l, 2 * n + 2))
                    nc.scalar.copy(ret_v[:, n, 0:512], ps[:, 6 + n % 2, :]).then_inc(ro_ev.sem, 1)

                def norm_square(n):
                    act.wait_ge(ro_ev.sem, ro_ev.at(l, n + 1))
                    act.wait_ge(m_sum.sem, m_sum.at(l, 3 + n - 1))
                    square(3 + n, n % 2, ret_v[:, n, :])

                def norm_root(n):
                    act.wait_ge(m_sum.sem, m_sum.at(l, 3 + n + 1))
                    nc.scalar.activation(halves(ret_root[:, n, :]), pair(4 + 2 * (n % 2)), ACT.Sqrt,
                                         bias=eps[:, 0:1], scale=1.0 / VD).then_inc(m_root.sem, 1)

                act.wait_ge(so_ev.sem, so_ev.at(l, 1))
                norm_square(0)
                norm_square(1)
                for h in range(HEADS):
                    act.wait_ge(qa_mm.sem, qa_mm.at(l, h + 1))
                    nc.scalar.copy(q_abss[:, h, :], ps[:, 2 * (h % 2) + 1, 0:NS])
                    nc.scalar.copy(q_abs[:, h, :], ps[:, 2 * (h % 2), :]).then_inc(qa_ev.sem, 1)
                    if h in (1, 3, 5, 7):
                        norm_root(h // 2)
                        if h // 2 + 2 < 4:
                            norm_square(h // 2 + 2)

                def exponential(n, j):
                    kind, h = ITEMS[n]
                    u = FIRST_UNIT[n] + j
                    act.wait_ge(sc_max.sem, sc_max.at(l, 2 * u + 2))
                    if n >= 2 and j == 0:
                        act.wait_ge(at_mm.sem, at_mm.at(l, FIRST_UNIT[n - 1]))
                    if kind == "p":
                        w = (j + 1) * P
                        src, dst = ps[:, j, 0:w], prob[:, n % 2, TRI_AT[j]:TRI_AT[j] + w]
                    else:
                        src, dst = pair(0), halves(prob[:, n % 2, 0:T])
                    c = slice(4 * (n % 2) + j, 4 * (n % 2) + j + 1)
                    nc.scalar.activation(dst, src, ACT.Exp, bias=neg_max[:, c], scale=MLA_SCALE,
                                         accum_out=exp_sum[:, c]).then_inc(sc_exp.sem, 1)

                def turned(n, j):
                    kind, h = ITEMS[n]
                    u = FIRST_UNIT[n] + j
                    act.wait_ge(at_mm.sem, at_mm.at(l, u + 1))
                    if n >= 2 and j == 0:
                        act.wait_ge(pv_mm.sem, pv_mm.at(l, n - 1))
                    if kind == "p":
                        nc.scalar.copy(pt[:, n % 2, TRI_AT[j]:TRI_AT[j] + (j + 1) * P], ps[:, 4 + u % 2, 0:(j + 1) * P])\
                            .then_inc(at_ev.sem, 1)
                    else:
                        nc.scalar.copy(pt[0:NS, n % 2, 512:512 + P], ps[0:NS, 6, 0:P])
                        nc.scalar.copy(pt[:, n % 2, 0:512], ps[:, 4 + u % 2, :]).then_inc(at_ev.sem, 1)

                units = [4 if kind == "p" else 1 for kind, _ in ITEMS] + [0]
                for j in range(4):
                    exponential(0, j)
                for n in range(len(ITEMS)):
                    for j in range(max(units[n], units[n + 1])):
                        if j < units[n + 1]:
                            exponential(n + 1, j)
                        if j < units[n]:
                            turned(n, j)
                    if n < 4:
                        ret_out(l, n)
                    if n and ITEMS[n - 1][0] == "p" and ITEMS[n - 1][1] % 2:
                        heads_high(l, ITEMS[n - 1][1] // 2)
                heads_high(l, 3)
                act.wait_ge(uv_mm.sem, uv_mm.at(l, 5))
                nc.scalar.copy(mla_hi[:, :, 512:T], ps[:, 6, 0:4 * NS].rearrange("p (a n) -> p a n", a=4))\
                    .then_inc(uv_hi.sem, 1)
                act.wait_ge(stored.sem, stored.at(l, 64))
                out_tiles(l, 1, MIX_C0 + OUT_C0, 1, KD, o_mix)

            def ret_out(l, n):
                act.wait_ge(ret_prod.sem, ret_prod.at(l, 2 * n + 2))
                nc.scalar.copy(ret_hi[:, n, :], ret_v[:, n, :]).then_inc(ret_high.sem, 1)

            def heads_high(l, p):
                act.wait_ge(uv_mm.sem, uv_mm.at(l, p + 1))
                nc.scalar.copy(mla_hi[:, p, 0:512], ps[:, 7, :]).then_inc(uv_hi.sem, 1)

            act.wait_ge(filled.sem, 3)
            act.wait_ge(c_in.sem, 16)
            nc.scalar.activation(c_all[:, :, :], c_all[:, :, :], ACT.Silu).then_inc(c_act.sem, 1)
            with act.Fori(0, DEPTH) as l:
                ffn(l, 0)
                mixer(l)
                ffn(l, 1)

        @block.vector
        def _(dve):
            v_ = nc.vector
            GROUPS = (slice(0, NP_), slice(NP_, T))

            v_.memset(ones[:, :], 1.0).then_inc(filled.sem, 1)
            v_.memset(eps[:, :], EPS).then_inc(filled.sem, 1)
            v_.memset(neg_row[:, :], NEG / P).then_inc(filled.sem, 1)
            for k in range(2):
                v_.memset(scratch[:, 12 + k:13 + k], 0.0).then_inc(up_lo.sem, 1)
            for k in range(4):
                v_.memset(scratch[:, 16 + k:17 + k], 0.0).then_inc(up_mul.sem, 1)
                v_.memset(scratch[:, 20 + k:21 + k], 0.0).then_inc(up_out.sem, 1)
            v_.memset(wide_rinv[:, T:TW], 1.0).then_inc(filled.sem, 1)

            def ada_group(l, land_n, n0, done0, cols, before_group=0, first_ffn=False):
                for t in range(ADA_RING):
                    if before_group is None:
                        dve.wait_ge(ada_landed[t].sem, 16 * (land_n + 1))
                    else:
                        dve.wait_ge(ada_landed[t].sem, ada_landed[t].at(l, land_n * 16 + 16))
                    if t == 0 and before_group is None:
                        if cols:
                            dve.wait_ge(columns.sem, cols)
                    elif t == 0:
                        dve.wait_ge(columns.sem, columns.at(l, cols))
                        dve.wait_ge(up_lo.sem, up_lo.at(l, FT if first_ffn else 2 * FT))
                    for v in range(2):
                        if before_group is None:
                            if done0 or t:
                                dve.wait_ge(ada_done.sem, 2 * (done0 + t) + v - 1)
                        else:
                            dve.wait_ge(ada_done.sem, ada_done.at(l, 2 * done0 + (2 * t + v - 1)))
                        v_.tensor_tensor_reduce(junk[v], ada_w[:, t, :], c_all[:, v, :], 1.0, 0.0, ALU.mult,
                                                ALU.add, acc[:, v, t:t + 1]).then_inc(ada_done.sem, 1)
                if before_group is None:
                    dve.wait_ge(ada_done.sem, 2 * (done0 + ADA_RING))
                else:
                    dve.wait_ge(ada_done.sem, ada_done.at(l, 2 * done0 + 2 * ADA_RING))
                for v in range(2):
                    bias = ada_b[:, bass.ds(before_col(l, before_group, done0), ADA_RING)]
                    v_.tensor_tensor(mods[:, v, bass.ds(n0, ADA_RING)], acc[:, v, :], bias, ALU.add)\
                        .then_inc(columns.sem, 1)

            def before_col(l, before_group, done0):
                return done0 if before_group is None else l * MODS + 16 + done0

            def pre_columns(l, j, layer_of):
                for v in range(2):
                    c = (3 * j + 1) * KD
                    v_.scalar_tensor_tensor(out=mul_pre[:, j, v, :], in0=mods[:, v, c:c + KD], scalar=1.0,
                                            in1=g_pre[:, bass.ds(layer_of * 3 * KD + j * KD, KD)],
                                            op0=ALU.add, op1=ALU.mult).then_inc(columns.sem, 1)

            def post_columns(l, j):
                for v in range(2):
                    c = (3 * j + 2) * KD
                    v_.scalar_tensor_tensor(out=mul_post[:, j, v, :], in0=mods[:, v, c:c + KD],
                                            scalar=1.0 if j == 1 else 0.5,
                                            in1=g_post[:, bass.ds(l * 3 * KD + j * KD, KD)],
                                            op0=ALU.mult, op1=ALU.mult).then_inc(columns.sem, 1)

            def invert(l, root_sig, inv_sig, n):
                dve.wait_ge(root_sig.sem, root_sig.at(l, n + 1))
                v_.reciprocal(rinv[:, :], root[:, :]).then_inc(inv_sig.sem, 1)
                dve.wait_ge(inv_sig.sem, inv_sig.at(l, n + 1))

            def pre_norm(l, j):
                invert(l, rooted, inverted, 2 * j)
                dve.wait_ge(columns.sem, columns.at(l, COL_A))

                def low(m):
                    dve.wait_ge(h_high.sem, h_high.at(l, H_AT[j] + 2 * m + 2))
                    for v, n in enumerate(GROUPS):
                        c = 3 * j * KD + m
                        v_.scalar_tensor_tensor(out=h_lo[:, m, n], in0=tmp_v[:, m % 2, n], scalar=mods[:, v, c:c + 1],
                                                in1=h_hi[:, m, n].bitcast(F32), op0=ALU.add, op1=ALU.subtract)\
                            .then_inc(h_ready.sem, 1)

                for m in range(KD):
                    if m >= 2:
                        dve.wait_ge(h_ready.sem, h_ready.at(l, H_AT[j] + 2 * m - 2))
                    for v, n in enumerate(GROUPS):
                        v_.scalar_tensor_tensor(out=tmp_v[:, m % 2, n], in0=x[:, m, n], scalar=mul_pre[:, j, v, m:m + 1],
                                                in1=rinv[:, n], op0=ALU.mult, op1=ALU.mult).then_inc(h_scaled.sem, 1)
                    if m:
                        low(m - 1)
                low(KD - 1)

            def pre_scale(l, j):
                dve.wait_ge(columns.sem, columns.at(l, COL_A if j else 0))
                dve.wait_ge(h_high.sem, h_high.at(l, H_AT[j] + 2))
                for v in range(2):
                    c = 3 * j * KD
                    v_.tensor_tensor(h_lo[:, :, T + 2 * v:T + 2 * v + 2],
                                     mods[:, v, c:c + KD].unsqueeze(2).to_broadcast([P, KD, 2]),
                                     h_hi[:, :, T + 2 * v:T + 2 * v + 2].bitcast(F32),
                                     ALU.subtract).then_inc(h_ready.sem, 1)
                for m in range(KD):
                    dve.wait_ge(h_high.sem, h_high.at(l, H_AT[j] + 2 + 2 * m + 2))
                    for v, n in enumerate(GROUPS):
                        v_.scalar_tensor_tensor(out=h_lo[:, m, n], in0=x[:, m, n], scalar=mul_pre[:, j, v, m:m + 1],
                                                in1=h_hi[:, m, n].bitcast(F32), op0=ALU.mult, op1=ALU.subtract)\
                            .then_inc(h_ready.sem, 1)
                dve.wait_ge(rooted.sem, rooted.at(l, 2 * j + 1))
                v_.reciprocal(rinv[:, :], root[:, :]).then_inc(inverted.sem, 1)

            def post_norm(l, j, o_buf):
                invert(l, rooted, inverted, 2 * j + 1)
                dve.wait_ge(columns.sem, columns.at(l, COL_A + (COL_B if j == 2 else 0)))

                def add(m):
                    dve.wait_ge(x_prod.sem, x_prod.at(l, j * 16 + 2 * m + 2))
                    v_.tensor_tensor(x[:, m, :], x[:, m, :], tmp_v[:, m % 2, :], ALU.add).then_inc(x_new[m % 2].sem, 1)

                for m in range(KD):
                    if m >= 2:
                        dve.wait_ge(x_new[m % 2].sem, x_new[m % 2].at(l, j * (KD // 2) + m // 2))
                    for v, n in enumerate(GROUPS):
                        v_.scalar_tensor_tensor(out=tmp_v[:, m % 2, n], in0=o_buf[:, m, n], scalar=mul_post[:, j, v, m:m + 1],
                                                in1=rinv[:, n], op0=ALU.mult, op1=ALU.mult).then_inc(x_prod.sem, 1)
                    if m % 2:
                        add(m - 1)
                add(KD - 1)

            def ffn(l, s):
                pre_scale(l, 2 * s)
                with dve.Fori(0, FT // 2) as i:
                    for f in range(2):
                        n = s * FT + i * 2 + f
                        dve.wait_ge(inverted.sem, inverted.at(l, 4 * s + 1))
                        dve.wait_ge(up_mul.sem, up_mul.at(l, 2 * n - 2))
                        dve.wait_ge(w_used.sem, w_used.at(l, FFN_C[s] + i * 4 + 2 * f + 1))
                        v_.tensor_tensor(halves(wide_s[:, f, :]), wide_pair(4 * f), halves(wide_rinv[:, :]), ALU.mult)\
                            .then_inc(up_out.sem, 1)
                        dve.wait_ge(up_lo.sem, up_lo.at(l, n - 1))
                        dve.wait_ge(w_used.sem, w_used.at(l, FFN_C[s] + i * 4 + 2 * f + 2))
                        v_.tensor_tensor(halves(wide_v[:, f, :]), wide_pair(4 * f + 2), halves(wide_rinv[:, :]), ALU.mult)\
                            .then_inc(up_out.sem, 1)
                        dve.wait_ge(up_silu.sem, up_silu.at(l, 2 * n + 2))
                        dve.wait_ge(up_out.sem, up_out.at(l, 2 * n + 2))
                        for v, at in enumerate(GROUPS):
                            v_.scalar_tensor_tensor(out=wide_v[:, f, at], in0=wide_v[:, f, at],
                                                    scalar=wide_v[:, f, T + 2 * v:T + 2 * v + 1], in1=wide_s[:, f, at],
                                                    op0=ALU.add, op1=ALU.mult).then_inc(up_mul.sem, 1)
                        dve.wait_ge(up_hi.sem, up_hi.at(l, n + 1))
                        at = bass.ds(i * 2 + f, 1)
                        v_.tensor_tensor(u_lo[:, at, :].rearrange("p a n -> p (a n)"), tmp_v[:, f, :],
                                         u_hi[:, at, :].rearrange("p a n -> p (a n)").bitcast(F32), ALU.subtract)\
                            .then_inc(up_lo.sem, 1)
                if s == 0:
                    with dve.Fori(0, ADA_A // ADA_RING) as i:
                        ada_group(l, i, 16 + i * ADA_RING, i * ADA_RING, i * 2, first_ffn=True)
                    dve.wait_ge(columns.sem, columns.at(l, 2 * ADA_A // ADA_RING))
                    post_columns(l, 0)
                    pre_columns(l, 1, l)
                    post_columns(l, 1)
                    pre_columns(l, 2, l)
                else:
                    g0 = ADA_A // ADA_RING
                    with dve.Fori(0, 2) as i:
                        ada_group(l, i + g0, 64 + i * ADA_RING, ADA_A + i * ADA_RING, i * 2 + COL_A)
                    with dve.Fori(0, 4) as i:
                        ada_group(l, i + (g0 + 2), i * ADA_RING, (ADA_A + 8) + i * ADA_RING, i * 2 + (COL_A + 4))
                    dve.wait_ge(columns.sem, columns.at(l, COL_A + 2 * ADA_B // ADA_RING))
                    post_columns(l, 2)
                    pre_columns(l, 0, l + 1)
                post_norm(l, 2 * s, o_ffn)

            def mixer(l):
                pre_norm(l, 1)
                v_.tensor_copy(gains[:, :], g_lat[:, bass.ds(l * 3, 3)]).then_inc(gains_in.sem, 1)
                dve.wait_ge(gains_in.sem, gains_in.at(l, 1))
                invert(l, m_root, m_inv, 0)
                for k in range(2):
                    v_.scalar_tensor_tensor(out=tmp_v[:, k, :], in0=zq[:, k, :], scalar=gains[:, k:k + 1], in1=rinv[:, :],
                                            op0=ALU.mult, op1=ALU.mult).then_inc(q_scaled.sem, 1)
                dve.wait_ge(q_scaled.sem, q_scaled.at(l, 2))
                invert(l, m_root, m_inv, 1)
                v_.scalar_tensor_tensor(out=kv[:, :], in0=kv[:, :], scalar=gains[:, 2:3], in1=rinv[:, :],
                                        op0=ALU.mult, op1=ALU.mult).then_inc(kv_ready.sem, 1)
                for k in range(2):
                    dve.wait_ge(q_high.sem, q_high.at(l, k + 1))
                    v_.tensor_tensor(qn_lo[:, k, :], tmp_v[:, k, :], qn_hi[:, k, :].bitcast(F32), ALU.subtract)\
                        .then_inc(q_low.sem, 1)

                turns = [0]

                def turn(out, in0, in1, op):
                    v_.tensor_tensor(out, in0, in1, op).then_inc(rope.sem, 1)
                    turns[0] += 1

                def turned_so_far():
                    dve.wait_ge(rope.sem, rope.at(l, turns[0]))

                def rotate(t, swapped):
                    turn(tmp_v[:, 0, :], t, rope_tab[:, 2, :], ALU.mult)
                    turn(tmp_v[:, 1, :], swapped, rope_tab[:, 3, :], ALU.mult)
                    turned_so_far()
                    turn(t, tmp_v[:, 0, :], tmp_v[:, 1, :], ALU.add)

                dve.wait_ge(q_low.sem, q_low.at(l, 2))
                dve.wait_ge(tables.sem, tables.at(l, 32))
                dve.wait_ge(z_ev.sem, z_ev.at(l, Z_EARLY))
                rotate(kpe[:, :], kpe_swap[:, :])
                for g in range(2):
                    dve.wait_ge(z_ev.sem, z_ev.at(l, Z_EARLY + 4 * g + 4))
                    for t in (ret_q, ret_k):
                        a1, a2 = t[:, 2 * g, :], t[:, 2 * g + 1, :]
                        cos, sin = rope_tab[:, 0, :], rope_tab[:, 1, :]
                        dve.wait_ge(rope.sem, rope.at(l, turns[0]))
                        turn(tmp_s[:, 0, :], a1, cos, ALU.mult)
                        turn(tmp_s[:, 1, :], a2, sin, ALU.mult)
                        turn(tmp_v[:, 0, :], a1, sin, ALU.mult)
                        turn(tmp_v[:, 1, :], a2, cos, ALU.mult)
                        dve.wait_ge(rope.sem, rope.at(l, turns[0]))
                        for hh in range(4):
                            r = slice(32 * hh, 32 * hh + 32)
                            pair_tile, row = 2 * g + hh // 2, 64 * (hh % 2)
                            turn(t[row:row + 32, pair_tile, :], tmp_s[r, 0, :], tmp_s[r, 1, :], ALU.subtract)
                            turn(t[row + 32:row + 64, pair_tile, :], tmp_v[r, 1, :], tmp_v[r, 0, :], ALU.add)
                dve.wait_ge(uq_ev.sem, uq_ev.at(l, 8))
                for g in range(2):
                    turned_so_far()
                    rotate(q_pe[:, g, :], q_pe_swap[:, g, :])

                v_.tensor_tensor(q_cross[:, :, :, :], ret_q[:, :, 512:T].unsqueeze(2).to_broadcast([P, 4, 2, NS]),
                                 cross[:, :, :, :], ALU.mult).then_inc(ss_mul.sem, 1)
                dve.wait_ge(kt_mm.sem, kt_mm.at(l, 1))
                v_.tensor_tensor(k_toks[:, :, :].rearrange("p g (h d) -> p (g h) d", h=2),
                                 ps[0:NS, 5, :].rearrange("p (g d) -> p g d", g=HEADS),
                                 k_decays[:, :].unsqueeze(2).to_broadcast([NS, HEADS, RDK]), ALU.mult)\
                    .then_inc(kt_ev.sem, 1)
                dve.wait_ge(ss_mm.sem, ss_mm.at(l, 1))
                dve.wait_ge(decay_in.sem, decay_in.at(l, 16))
                v_.tensor_tensor(ret_ss[:, :, :].rearrange("p (i g) n -> p g i n", g=2),
                                 ps[0:NS, 0:2, 0:4 * NS].rearrange("p g (i n) -> p g i n", i=4),
                                 decay[0:NS, :, 0:NS].rearrange("p (i g) n -> p g i n", g=2), ALU.mult)\
                    .then_inc(ss_mul.sem, 1)
                for h in range(HEADS):
                    if h:
                        dve.wait_ge(ro_mm.sem, ro_mm.at(l, h))
                    for b in range(4):
                        dve.wait_ge(rs_mm.sem, rs_mm.at(l, 4 * h + b + 1))
                        w = 512 - b * P
                        v_.tensor_tensor(ret_st[:, b, 0:w], ps[:, b, 0:w], decay[:, h, 0:w], ALU.mult)\
                            .then_inc(rs_mul.sem, 1)
                    i = h // 2
                    if h % 2 == 0:
                        dve.wait_ge(kt_mm.sem, kt_mm.at(l, 2 + i))
                        if i:
                            dve.wait_ge(st_mm.sem, st_mm.at(l, i))
                        v_.tensor_tensor(k_tok[:, :, :].rearrange("p b (h d) -> p b h d", h=2),
                                         ps[:, 4, :].rearrange("p (b h d) -> p b h d", b=4, h=2),
                                         k_decay[:, i, :, :].unsqueeze(3).to_broadcast([P, 4, 2, RDK]), ALU.mult)\
                            .then_inc(kt_ev.sem, 1)
                    else:
                        dve.wait_ge(st_mm.sem, st_mm.at(l, i + 1))
                        for hh in range(2):
                            r = slice(64 * hh, 64 * hh + 64)
                            v_.tensor_copy(state_p[r, i, :], ps[r, 5, hh * VD:(hh + 1) * VD]).then_inc(st_ev.sem, 1)
                            v_.scalar_tensor_tensor(out=state_in[r, i, :], in0=state_in[r, i, :],
                                                    scalar=state_decay[r, i:i + 1],
                                                    in1=ps[r, 5, P + hh * VD:P + (hh + 1) * VD],
                                                    op0=ALU.mult, op1=ALU.add).then_inc(st_ev.sem, 1)

                dve.wait_ge(ro_mm.sem, ro_mm.at(l, HEADS))
                v_.tensor_copy(cache_kv[:, PAST:T], kv[:, 512:T]).then_inc(cache_new.sem, 1)
                v_.tensor_copy(cache_pe[:, PAST:T], kpe[:, 512:T]).then_inc(cache_new.sem, 1)
                dve.wait_ge(rope.sem, rope.at(l, 57))
                for g in range(2):
                    v_.tensor_tensor(q_pes[:, g, :, :], q_pe[:, g, 512:T].unsqueeze(1).to_broadcast([P, 4, NS]),
                                     own_head[:, :, :], ALU.mult).then_inc(cache_new.sem, 1)

                def ret_prods(n):
                    dve.wait_ge(m_root.sem, m_root.at(l, 2 + n + 1))
                    if n:
                        dve.wait_ge(ret_prod.sem, ret_prod.at(l, 2 * n))
                    v_.reciprocal(rinv[:, :], ret_root[:, n, :]).then_inc(m_inv.sem, 1)
                    dve.wait_ge(m_inv.sem, m_inv.at(l, 2 + n + 1))
                    v_.tensor_tensor(ret_v[:, n, :], ret_v[:, n, :], rinv[:, :], ALU.mult).then_inc(ret_prod.sem, 1)
                    dve.wait_ge(ret_prod.sem, ret_prod.at(l, 2 * n + 1))
                    v_.tensor_tensor(ret_v[:, n, :], ret_v[:, n, :], ret_g[:, n, :], ALU.mult).then_inc(ret_prod.sem, 1)

                def ret_lows(n):
                    dve.wait_ge(ret_high.sem, ret_high.at(l, n + 1))
                    v_.tensor_tensor(ret_lo[:, n, :], ret_v[:, n, :], ret_hi[:, n, :].bitcast(F32), ALU.subtract)\
                        .then_inc(ret_low.sem, 1)

                dve.wait_ge(m_sum.sem, m_sum.at(l, 7))
                for g in range(4):
                    v_.tensor_scalar(own_keys[g][:, 0:NP_], kpe[:, 0:NP_], own_head[:, g, 0:1], None, ALU.mult)\
                        .then_inc(own_in.sem, 1)

                def maximum(n, j):
                    kind, h = ITEMS[n]
                    u = FIRST_UNIT[n] + j
                    c = slice(4 * (n % 2) + j, 4 * (n % 2) + j + 1)
                    dve.wait_ge(sc_mm.sem, sc_mm.at(l, u + 1))
                    if kind == "p":
                        v_.reduce_max(row_max[:, c], ps[:, j, 0:(j + 1) * P], AX.X).then_inc(sc_max.sem, 1)
                    else:
                        v_.tensor_reduce(row_max[:, c], pair(0), AX.XY, ALU.max).then_inc(sc_max.sem, 1)
                    dve.wait_ge(sc_max.sem, sc_max.at(l, 2 * u + 1))
                    v_.tensor_scalar(neg_max[:, c], row_max[:, c], -MLA_SCALE, None, ALU.mult).then_inc(sc_max.sem, 1)

                def normal(u):
                    n = max(i for i in range(len(ITEMS)) if FIRST_UNIT[i] <= u)
                    j = u - FIRST_UNIT[n]
                    at, w = (TRI_AT[j], (j + 1) * P) if ITEMS[n][0] == "p" else (0, T)
                    c = slice(4 * (n % 2) + j, 4 * (n % 2) + j + 1)
                    dve.wait_ge(sc_exp.sem, sc_exp.at(l, u + 1))
                    v_.reciprocal(inv_sum[:, c], exp_sum[:, c]).then_inc(sc_norm.sem, 1)
                    dve.wait_ge(sc_norm.sem, sc_norm.at(l, 2 * u + 1))
                    v_.tensor_scalar(prob[:, n % 2, at:at + w], prob[:, n % 2, at:at + w], inv_sum[:, c], None, ALU.mult)\
                        .then_inc(sc_norm.sem, 1)

                def latents_out(n):
                    kind, h = ITEMS[n]
                    dve.wait_ge(pv_mm.sem, pv_mm.at(l, n + 1))
                    if kind == "p":
                        v_.tensor_copy(o_lat[:, h % 2, :], ps[:, 6, :]).then_inc(pv_ev.sem, 1)
                    else:
                        v_.tensor_copy(o_lats[:, 4 * h:4 * h + 4, :], ps[:, 6, 0:P].rearrange("p (h n) -> p h n", h=4))\
                            .then_inc(pv_ev.sem, 1)

                def heads_low(p):
                    dve.wait_ge(uv_hi.sem, uv_hi.at(l, p + 1))
                    v_.tensor_tensor(mla_lo[:, p, 0:512], ps[:, 7, :], mla_hi[:, p, 0:512].bitcast(F32), ALU.subtract)\
                        .then_inc(uv_lo.sem, 1)

                for n in range(len(ITEMS)):
                    if n >= 2:
                        latents_out(n - 2)
                    for j in range(4 if ITEMS[n][0] == "p" else 1):
                        maximum(n, j)
                        if FIRST_UNIT[n] + j:
                            normal(FIRST_UNIT[n] + j - 1)
                        if j == 0 and n:
                            if n >= 3 and ITEMS[n - 3][0] == "p" and ITEMS[n - 3][1] % 2:
                                heads_low(ITEMS[n - 3][1] // 2)
                    if 2 <= n < 6:
                        ret_lows(n - 2)
                    if n < 4:
                        ret_prods(n)
                normal(SU - 1)
                latents_out(len(ITEMS) - 2)
                latents_out(len(ITEMS) - 1)
                heads_low(3)
                dve.wait_ge(uv_hi.sem, uv_hi.at(l, 5))
                v_.tensor_tensor(mla_lo[:, :, 512:T], ps[:, 6, 0:4 * NS].rearrange("p (a n) -> p a n", a=4),
                                 mla_hi[:, :, 512:T].bitcast(F32), ALU.subtract).then_inc(uv_lo.sem, 1)
                post_norm(l, 1, o_mix)

            dve.wait_ge(c_act.sem, 1)
            dve.wait_ge(const_in.sem, 16 * N_CONST)
            for i in range(4):
                ada_group(0, i, i * ADA_RING, i * ADA_RING, 2 * i, None)
            dve.wait_ge(columns.sem, 8)
            pre_columns(0, 0, 0)
            dve.wait_ge(x_in.sem, 16)
            for k in range(KD):
                v_.memset(scratch[:, 4 + k:5 + k], 0.0).then_inc(x_new[k % 2].sem, 1)
            with dve.Fori(0, DEPTH) as l:
                ffn(l, 0)
                mixer(l)
                ffn(l, 1)


OUTS = {"y": (P, KD, T), "kv": (DEPTH, P, T), "kpe": (DEPTH, ROPE, T),
        "state_p": (DEPTH, P, 4, VD), "state_s": (DEPTH, P, 4, VD)}


def tables():
    pos = np.arange(T, dtype=np.float32)
    p = np.arange(P)

    def angles(half, i):
        inv = np.float32(10000.0) ** (-np.arange(half, dtype=np.float32) / np.float32(half))
        return inv.astype(np.float32)[i][:, None] * pos[None, :]

    ret, mla = angles(32, p % 32), angles(16, p % 16)
    sign = np.where(p % 32 < 16, -1.0, 1.0)[:, None]
    rope = np.stack([np.cos(ret), np.sin(ret), np.cos(mla), sign * np.sin(mla)], 1).astype(np.float32)
    log_g = np.log1p(-np.exp2(-5.0 - np.arange(HEADS)))
    j = np.arange(512)
    diff = j[None, None, :] - p[:, None, None]
    decay = np.where(diff >= 0, np.exp(np.maximum(diff, 0) * log_g[None, :, None]), 0.0) * RET_SCALE
    head = np.arange(HEADS).reshape(4, 2)
    tok = (np.arange(4)[None, :] * P + p[:, None])
    k_decay = np.exp((511 - tok)[:, None, :, None] * log_g[head][None, :, None, :]) * RET_SCALE
    k_decays = np.exp((NS - 1 - np.arange(NS))[:, None] * log_g[None, :]) * RET_SCALE
    of_row = head[:, p // 64].T
    cross = np.exp((np.arange(NS) + 1.0)[None, None, :] * log_g[of_row][:, :, None])
    own = (p[:, None] // 64 == np.arange(2))[:, None, :, None]
    cross = np.where(own, cross[:, :, None, :], 0.0)
    own = (p[:, None] // 32 == np.arange(4))[:, :, None]
    state_decay = np.exp(NS * log_g[of_row])
    same = (p[:, None] // VD == p[None, :] // VD)
    return {"rope": rope, "decay": decay, "k_decay": k_decay, "k_decays": k_decays, "cross": cross,
            "state_decay": state_decay, "half_ones": same, "own_head": np.broadcast_to(own, (P, 4, NS)), "ident": np.eye(P)}


def tiles(w, n_k, n_c):
    w = w.reshape(*w.shape[:-2], n_k, P, n_c, P)
    return np.moveaxis(w, -2, -4).swapaxes(-2, -3)


def kernel(**inputs):
    import concourse.bacc as _bacc
    from concourse.bass_utils import run_bass_kernel_spmd as _run

    f = {k: np.asarray(v) for k, v in inputs.items()}
    L = DEPTH

    def feature_major(t):
        return t.T.reshape(KD, P, T).transpose(1, 0, 2)

    a = {k: np.ascontiguousarray(v, dtype=np.float32) for k, v in tables().items()}
    a["x"] = feature_major(np.concatenate([f["x_prompt"][0], f["x_sample"][0]], 0))
    a["c"] = np.stack([f["c_prompt"][0], f["c_sample"][0]])

    ada = f["ada_w"].transpose(0, 2, 1).reshape(L * MODS, P, D)
    a["ada"] = np.concatenate([ada, ada[:16]], 0)
    bias = f["ada_b"].reshape(L * MODS, P)
    a["ada_b"] = np.concatenate([bias, bias[:16]], 0).T
    pre = f["norm_pre"].reshape(L * 3 * KD, P)
    a["g_pre"] = np.concatenate([pre, pre[:KD]], 0).T
    a["g_post"] = f["norm_post"].reshape(L * 3 * KD, P).T
    a["g_lat"] = np.concatenate([f["q_norm"].reshape(L, 2, P), f["kv_norm"].reshape(L, 1, P)], 1).reshape(L * 3, P).T

    w1, w3 = (tiles(f[n], KD, FT) for n in ("ffn_w1", "ffn_w3"))
    a["w_up"] = np.stack([w1, w3], 3).reshape(L * 2 * UP_C, P, KD * P)
    w2 = tiles(f["ffn_w2"], FT, KD)
    w2 = w2.reshape(L, 2, KD, P, 2, DN_T * P).transpose(0, 1, 2, 4, 3, 5)
    a["w_dn"] = w2.reshape(L * 2 * DN_C, P, DN_T * P)

    q0, kv0, pe0, r0 = 0, Q_RANK, Q_RANK + KV_RANK, Q_RANK + KV_RANK + ROPE
    swap = np.r_[ROPE // 2:ROPE, 0:ROPE // 2]
    cols = [np.arange(q0, pe0), np.tile(pe0 + np.arange(ROPE), 4), np.tile(pe0 + swap, 4)]
    n_ret = HEADS * RDK
    halves_first = np.concatenate([
        (np.arange(HEADS)[:, None] * RDK + s * 32 + np.arange(32)[None, :]).ravel() for s in range(2)])
    parts = [r0 + halves_first, r0 + n_ret + halves_first, r0 + 2 * n_ret + np.arange(n_ret),
             r0 + 3 * n_ret + np.arange(n_ret)]
    q_cols, k_cols, v_cols, g_cols = ([part[i * P:(i + 1) * P] for i in range(4)] for part in parts)
    for g in range(2):
        cols += [q_cols[g], q_cols[g + 2], k_cols[g], k_cols[g + 2]]
    for g in range(2):
        cols += [v_cols[2 * g], v_cols[2 * g + 1], g_cols[2 * g], g_cols[2 * g + 1]]
    w_in = tiles(f["w_in"][:, :, np.concatenate(cols)], KD, Z_C).reshape(L, Z_C, P, KD * P)
    per = NOPE + ROPE
    heads = np.arange(HEADS)[:, None] * per
    uq_cols = np.concatenate([(heads + np.arange(NOPE)).ravel(), (heads + NOPE + np.arange(ROPE)).ravel(),
                              (heads + NOPE + swap).ravel()])
    uq = tiles(f["w_uq"][:, :, uq_cols], 2, 8)
    uq = uq.reshape(L, 2, 4, P, 2 * P).transpose(0, 1, 3, 2, 4).reshape(L, 2, P, KD * P)
    uk = f["w_uk"].transpose(0, 2, 1).reshape(L, 4, P, P).transpose(0, 2, 1, 3).reshape(L, P, 4 * P)
    ukv = np.concatenate([uk, f["w_uv"]], 2)[:, None]
    n_mla = HEADS * VD
    w_out = np.concatenate([f["w_out"][:, n_mla:], f["w_out"][:, :n_mla]], 1)
    w_out = tiles(w_out, KD, KD).reshape(L, KD, P, KD * P)
    a["w_mix"] = np.concatenate([w_in, uq, ukv, w_out], 1).reshape(L * MIX_C, P, KD * P)

    a["state"] = f["state_ret"][:, 0].reshape(L, 4, P, VD).transpose(0, 2, 1, 3)
    cache, pe = f["cache_kv_latent"][:, 0], f["cache_k_rope"][:, 0]
    a["cache_kv"] = cache.transpose(0, 2, 1)
    a["cache_pe"] = np.tile(pe.transpose(0, 2, 1), (1, 4, 1))
    a["cache_tok"] = cache.reshape(L, 4, P, KV_RANK).transpose(0, 2, 1, 3)

    nc = _bacc.Bacc("TRN2", target_bir_lowering=False, num_devices=1)
    arrays = {f"in_{n}": np.ascontiguousarray(v) for n, v in a.items()}
    ins = {n: nc.dram_tensor(f"in_{n}", arrays[f"in_{n}"].shape, F32, kind="ExternalInput").ap() for n in a}
    outs = {n: nc.dram_tensor(f"out_{n}", shape, F32, kind="ExternalOutput").ap() for n, shape in OUTS.items()}
    streaming_trunk(nc, ins, outs)
    r = _run(nc, [arrays], core_ids=[0]).results[0]
    y, kv, kpe, st_p, st_s = (np.asarray(r[f"out_{n}"]) for n in ("y", "kv", "kpe", "state_p", "state_s"))
    y = y.transpose(1, 0, 2).reshape(D, T).T
    kv, kpe = kv.transpose(0, 2, 1)[:, None], kpe.transpose(0, 2, 1)[:, None]

    def state_of(s):
        s = s.transpose(0, 2, 1, 3)
        return np.ascontiguousarray(s.reshape(L, 1, HEADS, RDK, VD))

    out = (y[None, :NP_], y[None, NP_:], kv[:, :, :NP_], kpe[:, :, :NP_], state_of(st_p),
           kv[:, :, NP_:], kpe[:, :, NP_:], state_of(st_s))
    return tuple(np.ascontiguousarray(t) for t in out)
```
